# Optimizing a Trainium2 kernel written in Bass

```python
import math
import jax, jax.numpy as jnp
from jax import lax
import numpy as np

D_MODEL = 1024
BATCH = 1
SEQ = 1024
DEPTH = 1
DEC_BATCH = 1
DEC_SEQ = 1024
PAST_LEN = 128

HEAD_DIM = 64
HEADS_PER_GROUP = 4
ATTN_PATTERNS = ((128, 1), (512, 4), (2048, 16))
N_ATTN_HEADS = HEADS_PER_GROUP * len(ATTN_PATTERNS)
ATTN_WIDTH = N_ATTN_HEADS * HEAD_DIM
ATTN_OUT_WIDTH = HEADS_PER_GROUP * HEAD_DIM
ROPE_DIM = HEAD_DIM // 4
ROPE_THETA = 500000.0
POOL_WINDOWS = (2, 4, 8, 16)
POOL_WIDTH = D_MODEL // 2
POOL_GROUP = POOL_WIDTH // len(POOL_WINDOWS)
IN_WIDTH = POOL_WIDTH + 3 * ATTN_WIDTH
D_FF = -(-8 * D_MODEL // (3 * 256)) * 256
BLOCK_Q = 64
NORM_EPS = 1e-6

kernel_name = "gated_pool_dilated_attn_encoder"

def rmsnorm(x, g):
    xf = x.astype(jnp.float32)
    y = xf * lax.rsqrt(jnp.mean(xf * xf, axis=-1, keepdims=True) + NORM_EPS) * g.astype(jnp.float32)
    return y.astype(x.dtype)

def partial_rope(t, pos):
    half = ROPE_DIM // 2
    inv = jnp.asarray(ROPE_THETA ** (-np.arange(half, dtype=np.float32) / half), dtype=jnp.float32)
    ang = pos[:, None] * inv[None, :]
    cos = jnp.cos(ang)[None, :, None, :]
    sin = jnp.sin(ang)[None, :, None, :]
    tf = t.astype(jnp.float32)
    x1 = tf[..., :half]
    x2 = tf[..., half:ROPE_DIM]
    rot = jnp.concatenate([x1 * cos - x2 * sin, x2 * cos + x1 * sin, tf[..., ROPE_DIM:]], axis=-1)
    return rot.astype(t.dtype)

def pool_mixer(u, maps, scale):
    B, S, _ = u.shape
    uf = u.astype(jnp.float32)
    c = jnp.pad(jnp.cumsum(uf, axis=1), ((0, 0), (1, 0), (0, 0)))
    pos = np.arange(S)
    outs = []
    for g, w in enumerate(POOL_WINDOWS):
        sl = slice(g * POOL_GROUP, (g + 1) * POOL_GROUP)
        lo = np.clip(pos - w // 2, 0, S)
        hi = np.clip(pos + w // 2, 0, S)
        cnt = jnp.asarray((hi - lo).astype(np.float32))[None, :, None]
        cg = c[..., sl]
        outs.append((cg[:, hi] - cg[:, lo]) / cnt - uf[..., sl])
    pooled = jnp.stack(outs, axis=2)
    mixed = jnp.einsum('bsgc,gcd->bsgd', pooled, maps.astype(jnp.float32)).reshape(B, S, POOL_WIDTH)
    return (mixed * scale.astype(jnp.float32)).astype(u.dtype)

def dilated_window_attention(q, k, v, window, dilation):
    B, S, H, E = q.shape
    d = dilation
    n = S // d
    R = (window // 2) // d
    qb = math.gcd(n, BLOCK_Q)
    nb = n // qb
    span = qb + 2 * R

    def to_sub(t):
        return t.reshape(B, n, d, H, E).transpose(0, 2, 1, 3, 4)

    qs = to_sub(q).reshape(B, d, nb, qb, H, E)
    pad = ((0, 0), (0, 0), (R, R), (0, 0), (0, 0))
    kp = jnp.pad(to_sub(k), pad)
    vp = jnp.pad(to_sub(v), pad)
    kidx = np.arange(nb)[:, None] * qb + np.arange(span)[None, :]
    kb = kp[:, :, kidx]
    vb = vp[:, :, kidx]
    s = jnp.einsum('bdnqhe,bdnkhe->bdnhqk', qs, kb, preferred_element_type=jnp.float32) * (E ** -0.5)
    rel = np.arange(span)[None, :] - R - np.arange(qb)[:, None]
    key_sub = kidx - R
    mask = (np.abs(rel) <= R)[None] & ((key_sub >= 0) & (key_sub < n))[:, None, :]
    s = jnp.where(jnp.asarray(mask)[None, None, :, None], s, -jnp.inf)
    m = jnp.max(s, axis=-1, keepdims=True)
    p = jnp.exp(s - m)
    den = jnp.sum(p, axis=-1, keepdims=True)
    o = jnp.einsum('bdnhqk,bdnkhe->bdnqhe', p, vb.astype(jnp.float32)) / den.transpose(0, 1, 2, 4, 3, 5)
    lse = (m + jnp.log(den))[..., 0].transpose(0, 1, 2, 4, 3)
    o = o.reshape(B, d, n, H, E).transpose(0, 2, 1, 3, 4).reshape(B, S, H, E)
    lse = lse.reshape(B, d, n, H).transpose(0, 2, 1, 3).reshape(B, S, H)
    return o, lse

def attention_branch(z_attn):
    B, S, _ = z_attn.shape
    q = z_attn[..., :ATTN_WIDTH].reshape(B, S, N_ATTN_HEADS, HEAD_DIM)
    k = z_attn[..., ATTN_WIDTH:2 * ATTN_WIDTH].reshape(B, S, N_ATTN_HEADS, HEAD_DIM)
    v = z_attn[..., 2 * ATTN_WIDTH:].reshape(B, S, N_ATTN_HEADS, HEAD_DIM)
    pos = jnp.arange(S, dtype=jnp.float32)
    q = partial_rope(q, pos)
    k = partial_rope(k, pos)
    outs, lses = [], []
    for g, (w, dil) in enumerate(ATTN_PATTERNS):
        hs = slice(g * HEADS_PER_GROUP, (g + 1) * HEADS_PER_GROUP)
        o, l = dilated_window_attention(q[:, :, hs], k[:, :, hs], v[:, :, hs], w, dil)
        outs.append(o)
        lses.append(l)
    outs = jnp.stack(outs, axis=0)
    alpha = jax.nn.softmax(jnp.stack(lses, axis=0), axis=0)
    merged = jnp.sum(alpha[..., None] * outs, axis=0).reshape(B, S, ATTN_OUT_WIDTH)
    return merged.astype(z_attn.dtype)

def encoder_forward(x, norm_mix, w_in, pool_maps, pool_scale, w_up_pool, w_up_attn, w_gate, b_gate,
                    w_out, norm_ffn, w_ffn_gate, w_ffn_up, w_ffn_down, norm_final):
    for l in range(DEPTH):
        h = rmsnorm(x, norm_mix[l])
        z = h @ w_in[l]
        a = pool_mixer(z[..., :POOL_WIDTH], pool_maps[l], pool_scale[l]) @ w_up_pool[l]
        b = attention_branch(z[..., POOL_WIDTH:]) @ w_up_attn[l]
        gates = jax.nn.sigmoid(h @ w_gate[l] + b_gate[l])
        g_a = gates[..., :D_MODEL]
        g_b = gates[..., D_MODEL:]
        x = x + (g_a * a + g_b * b) @ w_out[l]
        h = rmsnorm(x, norm_ffn[l])
        x = x + (jax.nn.silu(h @ w_ffn_gate[l]) * (h @ w_ffn_up[l])) @ w_ffn_down[l]
    return rmsnorm(x, norm_final)

def setup_inputs(seed: int = 0) -> dict:
    key = jax.random.key(seed)
    ks = jax.random.split(key, 18)
    f32 = jnp.float32

    def dense(k, shape, fan_in):
        return jax.random.normal(k, shape, f32) * (fan_in ** -0.5)

    def gain(k, shape):
        return 1.0 + 0.05 * jax.random.normal(k, shape, f32)

    return {
        "x_prompt": jax.random.normal(ks[0], (BATCH, SEQ, D_MODEL), f32),
        "x_sample": jax.random.normal(ks[1], (DEC_BATCH, DEC_SEQ, D_MODEL), f32),
        "norm_mix": gain(ks[2], (DEPTH, D_MODEL)),
        "w_in": dense(ks[3], (DEPTH, D_MODEL, IN_WIDTH), D_MODEL),
        "pool_maps": dense(ks[4], (DEPTH, len(POOL_WINDOWS), POOL_GROUP, POOL_GROUP), POOL_GROUP),
        "pool_scale": gain(ks[5], (DEPTH, POOL_WIDTH)),
        "w_up_pool": dense(ks[6], (DEPTH, POOL_WIDTH, D_MODEL), POOL_WIDTH),
        "w_up_attn": dense(ks[7], (DEPTH, ATTN_OUT_WIDTH, D_MODEL), ATTN_OUT_WIDTH),
        "w_gate": dense(ks[8], (DEPTH, D_MODEL, 2 * D_MODEL), D_MODEL),
        "b_gate": 0.02 * jax.random.normal(ks[9], (DEPTH, 2 * D_MODEL), f32),
        "w_out": dense(ks[10], (DEPTH, D_MODEL, D_MODEL), D_MODEL),
        "norm_ffn": gain(ks[11], (DEPTH, D_MODEL)),
        "w_ffn_gate": dense(ks[12], (DEPTH, D_MODEL, D_FF), D_MODEL),
        "w_ffn_up": dense(ks[13], (DEPTH, D_MODEL, D_FF), D_MODEL),
        "w_ffn_down": dense(ks[14], (DEPTH, D_FF, D_MODEL), D_FF),
        "norm_final": gain(ks[15], (D_MODEL,)),
    }

def reference(x_prompt, x_sample, norm_mix, w_in, pool_maps, pool_scale, w_up_pool, w_up_attn, w_gate, b_gate,
              w_out, norm_ffn, w_ffn_gate, w_ffn_up, w_ffn_down, norm_final):
    y_prompt = encoder_forward(x_prompt, norm_mix, w_in, pool_maps, pool_scale, w_up_pool, w_up_attn, w_gate,
                               b_gate, w_out, norm_ffn, w_ffn_gate, w_ffn_up, w_ffn_down, norm_final)
    y_sample = encoder_forward(x_sample, norm_mix, w_in, pool_maps, pool_scale, w_up_pool, w_up_attn, w_gate,
                               b_gate, w_out, norm_ffn, w_ffn_gate, w_ffn_up, w_ffn_down, norm_final)
    return (y_prompt, y_sample)


_drawn_inputs = setup_inputs


def setup_inputs(seed=0):
    import zlib

    import numpy as np

    out = dict(_drawn_inputs(seed))
    spreads = {}
    factors = {'b_gate': 8.0}
    for name, (base, spread) in spreads.items():
        noise = np.random.default_rng([zlib.crc32(name.encode()), seed]).standard_normal(out[name].shape)
        drawn = base * np.exp(spread * noise) if base else spread * noise
        out[name] = __import__('jax').numpy.asarray(drawn.astype(out[name].dtype))
    for name, factor in factors.items():
        out[name] = (out[name] * factor).astype(out[name].dtype)
    return out
```

```python
from contextlib import ExitStack

import numpy as np

import concourse.bass as bass
from concourse import mybir

F32 = mybir.dt.float32
F32R = mybir.dt.float32r
ALU = mybir.AluOpType
ACT = mybir.ActivationFunctionType
AX_X = mybir.AxisListType.X

P = 128
SEQS, T, D = 2, 1024, 1024
KD = D // P
TT = T // P
H2 = 512
HEAD, HPG, GROUPS = 64, 4, 3
DIL = (1, 4, 8)
RADIUS = 64
AW = HEAD * HPG * GROUPS
PW = 512
POOL_GROUPS = 4
FF = 2816
FF_TILES = FF // P
EPS = 1e-6
ROPE_HALF, THETA = 8, 500000.0
REC = 2 * HEAD + 4
UNITS = 2 * TT
BIG = 3.0e38

CREDIT = {"bank_full": 3, "w_ready": 1, "p_ready": 1, "y_sum": 1, "y_ready": 2, "x_added": 8,
          "out_stored0": 16, "out_stored1": 16}
N_V = (11, 8, 8)
PER_SEQ = {
    "ss_ready": 24, "std_ready": 24, "xn_ready": 16, "htmp_ready": 32, "hhi_ready": 32, "h_ready": 32,
    "rope_read": 24, "qk_ready": 24, "v_ready": sum(N_V), "s_read": 48, "negmax_ready": 48, "p_ready": 48,
    "pt_ready": 48, "o_ready": 48, "u_ready": 8, "pooled_ready": 4, "pool_hi_ready": 4, "pool_ready": 4,
    "mixed_ready": 8, "diff_ready": 8, "weight_ready": 8, "mtok_ready": 8, "mhi_ready": 4, "mT_ready": 4,
    "a_read": 16, "b_read": 16, "sig_ready": 76, "y_sum": 60, "yhi_ready": 60, "y_ready": 60,
    "x_added": 240, "fin_ready": 8, "bias_ready": 8,
}
DMA_SEMS = {"tab_in": 3, "gfin_in": 1}
DMA_SEMS.update({f"x_in{t}": 2 for t in range(TT)})
DMA_SEMS.update({f"rec_in{t}": 2 for t in range(4)})
DMA_SEMS.update({f"o_stored{n}": 12 for n in range(4)})
DMA_SEMS.update({"out_stored0": 4, "out_stored1": 4})
PER_SEQ.update(DMA_SEMS)


def due(name, s, n):
    step = 16 if name in DMA_SEMS else 1
    return s * (PER_SEQ[name] * step) + (CREDIT.get(name, 0) + n * step)


def v_tokens(g):
    if g:
        return [P * j for j in range(TT)]
    return [64 + P * j for j in range(7)] + [0, 128, 768, 896]


def window(g, b):
    if g == 0:
        if b == 0:
            return 0, 256, (7, 8), 1
        if b == TT - 1:
            return T - 256, 256, (9, 10), 2
        return P * b - 64, 256, (b - 1, b), 0
    if g == 1:
        r = b // 2
        return 256 * r, 256, (2 * r, 2 * r + 1), 1 + b % 2
    return P * b, P, (b,), 3


def phase_steps(g):
    if g == GROUPS - 1:
        return [(("u", j), k) for j in range(8) for k in range(KD)]
    tiles = [(("proj", g + 1, j), k) for j in range(8) for k in range(KD)]
    values = [(("proj", g + 1, 8 + v), k) for v in range(N_V[g + 1]) for k in range(KD)]
    steps, tiles = tiles[:2 * KD], tiles[2 * KD:]
    for n in range(len(tiles) // 4):
        steps += tiles[4 * n:4 * n + 4] + values[3 * n:3 * n + 3]
    return steps + values[len(tiles) // 4 * 3:]


def cut(g):
    steps = phase_steps(g)
    cost = [1 if job[0] == "proj" and job[2] >= 8 else 2 for job, _ in steps]
    total, parts, at_time = sum(cost), [[] for _ in range(3 * UNITS)], 0
    for step, c in zip(steps, cost):
        parts[at_time * 3 * UNITS // total].append(step)
        at_time += c
    return parts


PARTS = [p for g in range(3) for p in cut(g)]


def done(first, last):
    return [job for p in PARTS[max(first, 0):last + 1] for job, k in p if k == KD - 1]



class Plan:

    def __init__(self):
        self.fills = [0] * 8
        self.job, self.before = {}, {}
        self.reader = [("x_added", b + 1 - 8) for b in range(8)]
        self.norm(1)
        for j in range(8 + N_V[0]):
            self.proj(0, j)
        for n in range(GROUPS * UNITS):
            for h in range(2):
                self.take(("s", n, h), 4 + h, "s_read", n + 1)
            self.take(("pt", n), 6, "pt_ready", n + 1)
            self.take(("o", n), 7, "o_ready", n + 1)
            for part in PARTS[3 * n:3 * n + 3]:
                for job, k in part:
                    if k == 0 and job[0] == "proj":
                        self.proj(job[1], job[2])
                    elif k == 0:
                        self.take(job, job[1] % 4, "u_ready", job[1] + 1)
        for j in range(8):
            self.take(("mix", j), j, "mixed_ready", j + 1)
        for j in range(4):
            self.take(("mt", j), 4 + j, "mT_ready", j + 1)
        self.gate0 = list(self.fills)
        self.fills = [n + GATE_STEPS * GATE_FILLS for n in self.fills]
        self.reader = [("x_added", 16 * GATE_STEPS + b + 1 - 8) for b in range(8)]
        self.norm(2)
        self.ffn0 = list(self.fills)
        self.total = [n + FFN_STEPS * FFN_FILLS for n in self.fills]

    def norm(self, which):
        for t in range(TT):
            for half in range(2):
                self.take((f"n{which}", t, half), 2 * (t % 4) + half, "htmp_ready",
                          16 * (which - 1) + 2 * t + half + 1)

    def proj(self, g, j):
        bank = j % 2 if j < 8 or g and j >= 14 else 2 + j % 2
        if j < 8:
            self.take(("proj", g, j), bank, "rope_read", 8 * g + j + 1)
        else:
            self.take(("proj", g, j), bank, "v_ready", sum(N_V[:g]) + j - 8 + 1)

    def take(self, name, bank, sem, count):
        self.fills[bank] += 1
        self.job[name] = (bank, self.fills[bank])
        self.before[name] = self.reader[bank]
        self.reader[bank] = (sem, count)


GATE_STEPS, GATE_FILLS = 4, 4
FFN_STEPS, FFN_FILLS = FF_TILES // 2, 3
PLAN = Plan()
CHUNKS = []
for _g in range(GROUPS):
    CHUNKS += [(0, ("q", _g, 0), ("proj", _g, 2 if _g == 0 else 1)), (1, ("q", _g, 1), ("proj", _g, 3)),
               (2, ("v", _g, 0), ("proj", _g, 7 + N_V[_g])), (3, ("v", _g, 1), ("proj", _g, 7 + N_V[_g])),
               (0, ("k", _g, 0), ("proj", _g, 5)), (1, ("k", _g, 1), ("proj", _g, 7))]
CHUNKS += [(_g % 2, ("u", _g), ("u", 2 * _g + 1)) for _g in range(POOL_GROUPS)]
CHUNKS += [(0, ("maps", 0), ("mix", 3)), (1, ("maps", 1), ("mix", 7))]
F_PROJ, F_GATE, F_FFN = sum(c[0] == 0 for c in CHUNKS), 3, 2
D_PROJ = sum(c[0] == 2 for c in CHUNKS)
F_TOTAL = F_PROJ + F_GATE * GATE_STEPS + F_FFN * FFN_STEPS
D_TOTAL = D_PROJ + GATE_STEPS + FFN_STEPS
RAW_PROJ = len(CHUNKS) // 2
DVE_STEPS = 194
RAW_TOTAL = RAW_PROJ + 5 * GATE_STEPS + 3 * FFN_STEPS


def order(g, j):
    if g == 0 and j < 4:
        return j % 2, j // 2
    return j // 2, j % 2


class Chain:

    def __init__(self, eng, sem):
        self.eng, self.sem, self.base, self.n = eng, sem, 0, 0

    def link(self, ins):
        self.n += 1
        ins.then_inc(self.sem, 1)
        self.eng.wait_ge(self.sem, self.base + self.n)

    def enter(self, i, per):
        saved = (self.base, self.n)
        self.base, self.n = self.base + self.n + i * per, 0
        return saved

    def leave(self, saved, steps, per):
        assert self.n == per, ("steps in the loop", self.n, per)
        self.base, self.n = saved[0], saved[1] + steps * per


def encoder(nc, x, w_in, maps, w_up_pool, w_up_attn, w_gate, w_out, w_fg, w_fu, w_fd,
            norm_mix, norm_ffn, norm_final, pool_scale, b_gate,
            rope, masks, diag, ident, edge, scratch, out):
    ctx = ExitStack()
    with ctx:
        def sem(name):
            return ctx.enter_context(nc.semaphore(name))

        base = 16512

        def at(name, offset, shape, dt=F32):
            return nc.alloc_sbuf_tensor_at(name, [P] + shape, dt, offset=base + offset)

        h_hi, h_lo = at("h_hi", 0, [KD, T], F32R), at("h_lo", 32768, [KD, T], F32R)
        SLOT = 65536
        w_hi = [at(f"w_hi{s}", SLOT + 8192 * s, [D], F32R) for s in range(4)]
        w_lo = [at(f"w_lo{s}", SLOT + 8192 * s + 4096, [D], F32R) for s in range(4)]
        raw = [at(f"raw{r}", SLOT + 32768 + 4096 * r, [D]) for r in range(2)]
        XR = SLOT + 40960
        X = at("X", XR, [TT, D])
        qk = [at("qk_even", XR, [4, T]), at("qk_odd", XR + 16384, [4, T])]
        pool_hi, pool_lo = at("pool_hi", XR, [T], F32R), at("pool_lo", XR + 4096, [T], F32R)
        mtok = at("mtok", XR + 8192, [TT, 256])
        U = at("U", XR + 16384, [POOL_GROUPS, T])
        rec = at("rec", XR + 16384, [4, 6, REC])
        YR = XR + 32768
        y_hi = [at(f"y_hi{j}", YR + 8192 * j, [T], F32R) for j in range(2)]
        y_lo = [at(f"y_lo{j}", YR + 8192 * j + 4096, [T], F32R) for j in range(2)]
        rope_sb = at("rope_sb", YR, [2, T])
        masks_sb, diag_sb = at("masks_sb", YR + 8192, [3, 256]), at("diag_sb", YR + 11264, [P])
        MR = YR + 16384
        V = [at("V_even", MR, [11, 256]), at("V_odd", MR + 11264, [8, 256])]
        masked = at("masked", MR + 19456, [2, 256])
        prob = at("prob", MR + 21504, [2, 2, 256])
        probT = at("probT", MR + 25600, [4, P])
        r_sh, r_c, r_s = (at(f"rope_t{i}", MR + 27648 + 2048 * i, [H2]) for i in range(3))
        o_st = at("o_st", MR + 33792, [4, REC])
        pw0, pw1, pooled = (at("pw0", MR + 35904, [1040]), at("pw1", MR + 40064, [1040]),
                            at("pooled", MR + 44224, [T]))
        mix_hi, mix_lo = at("mix_hi", MR, [4, T], F32R), at("mix_lo", MR + 16384, [4, T], F32R)
        m_hi, m_lo = at("m_hi", MR + 32768, [2, T], F32R), at("m_lo", MR + 40960, [2, T], F32R)
        squares, xn = at("squares", MR, [D]), at("xn", MR + 4096, [2, D])
        n_tmp = at("n_tmp", MR + 12288, [2, 4, P])
        g_fin, fin = at("g_fin", MR + 16384, [D]), at("fin", MR + 20480, [2, D])
        SR = MR + 49152
        act_t = at("act_t", SR, [3, H2])
        off = [SR + 6144]

        def small(name, shape):
            n = int(np.prod(shape)) * 4
            o = off[0]
            off[0] = o + (n + 31) // 32 * 32
            return at(name, o, shape)

        ident_sb = small("ident_sb", [P])
        g_mix, g_ffn = small("g_mix", [KD]), small("g_ffn", [KD])
        p_scale, b_g, edge_sb = small("p_scale", [4]), small("b_g", [16]), small("edge_sb", [4, 16])
        zero, eps, b_now = small("zero", [1]), small("eps", [1]), small("b_now", [2])
        ss, std, rstd, mx = small("ss", [2]), small("std", [2]), small("rstd", [2]), small("mx", [2])
        mn, d3, e3, wd = small("mn", [4]), small("d3", [3, 4]), small("e3", [3, 4]), small("wd", [3, 4])
        den, rden, coef = small("den", [4]), small("rden", [4]), small("coef", [3, 4])
        assert base + off[0] <= nc.sbuf_usable_end
        ps = ctx.enter_context(nc.psum_tensor("ps", [P, 8, H2], F32))

        bank_full = [sem(f"bank_full{b}") for b in range(8)]
        raw_in = [sem(f"raw_in{r}") for r in range(2)]
        w_ready = [sem(f"w_ready{s}") for s in range(4)]
        w_hi_done, zeroed, eps_set, const_in, dve_chain = (
            sem(n) for n in ("w_hi_done", "zeroed", "eps_set", "const_in", "dve_chain"))
        sems = {name: sem(name) for name in PER_SEQ}
        (ss_ready, std_ready, xn_ready, htmp_ready, hhi_ready, h_ready, rope_read, qk_ready, v_ready, s_read,
         negmax_ready, p_ready, pt_ready, o_ready, u_ready, pooled_ready, pool_hi_ready, pool_ready, mixed_ready,
         diff_ready, weight_ready, mtok_ready, mhi_ready, mT_ready, a_read, b_read, sig_ready, y_sum, yhi_ready,
         y_ready, x_added, fin_ready, bias_ready, tab_in, gfin_in) = (
            sems[name] for name in PER_SEQ if not name[-1].isdigit())
        x_in = [sems[f"x_in{t}"] for t in range(TT)]
        rec_in = [sems[f"rec_in{t}"] for t in range(4)]
        o_stored = [sems[f"o_stored{t}"] for t in range(4)]
        out_stored = [sems[f"out_stored{t}"] for t in range(2)]

        def filled(s, b, n):
            return s * PLAN.total[b] + (CREDIT["bank_full"] + n)

        def split_by(s, slot, n):
            return s * (F_TOTAL if slot < 2 else D_TOTAL) + (CREDIT["w_ready"] + n)

        x_t = x.rearrange("s (t p) d -> s t p d", p=P)
        out_t = out.rearrange("s (t p) d -> s t p d", p=P)
        block = ctx.enter_context(nc.Block())

        @block.sync
        def _(sp):
            def cols(w):
                return w.rearrange("(k p) c -> p k c", p=P)

            w_in_c, w_gate_c = cols(w_in), cols(w_gate)
            upp_c, upa_c, fg_c, fu_c = cols(w_up_pool), cols(w_up_attn), cols(w_fg), cols(w_fu)
            w_out_r = w_out.rearrange("(k p) c -> k p c", p=P)
            w_fd_r = w_fd.rearrange("(k p) c -> k p c", p=P)
            maps_c = maps.rearrange("g c d -> c g d")

            def r3(r, n):
                return raw[r][:, 0:n * P].rearrange("p (k c) -> p k c", c=P)

            def raws_free(s, i, r):
                cols_split = sp.snap(s * F_TOTAL + (i * F_GATE + (F_PROJ + 1)))
                rows_split = sp.snap(s * D_TOTAL + (i + (D_PROJ + 1)))
                sp.wait_ge(w_ready[r], cols_split)
                sp.wait_ge(w_ready[2 + r], rows_split)

            with sp.Fori(0, SEQS) as s:
                done = [0] * 4
                for c, (slot, what, _) in enumerate(CHUNKS):
                    r, kind = c % 2, what[0]
                    if c < 2:
                        sp.wait_ge(w_ready[2 + c], split_by(s, 2 + c, 0))
                    else:
                        before = CHUNKS[c - 2][0]
                        sp.wait_ge(w_ready[before], split_by(s, before, done[before]))
                    done[slot] += 1
                    if kind == "u":
                        src, dst = w_in_c[:, :, P * what[1]:P * what[1] + P], r3(r, 8)
                    elif kind == "maps":
                        src, dst = maps_c[:, 2 * what[1]:2 * what[1] + 2, :], r3(r, 2)
                    elif kind == "v":
                        at_c = PW + 2 * AW + 256 * what[1]
                        src = w_in_c[:, 4 * what[2]:4 * what[2] + 4, at_c:at_c + 256]
                        dst = raw[r][:, :].rearrange("p (k c) -> p k c", c=256)
                    else:
                        at_c = PW + (AW if kind == "k" else 0) + 256 * what[1] + P * what[2]
                        src, dst = w_in_c[:, :, at_c:at_c + P], r3(r, 8)
                    sp.dma_start(dst, src).then_inc(raw_in[r], 16)
                with sp.Fori(0, GATE_STEPS) as i:
                    for j in range(2):
                        up, ga, gb = (3 * j) % 2, (3 * j + 1) % 2, (3 * j + 2) % 2
                        col = bass.ds(i * 256 + P * j, P)
                        if j == 0:
                            raws_free(s, i, 0)
                        else:
                            sp.wait_ge(w_ready[1], split_by(s, 1, F_PROJ + i * F_GATE + 1))
                        sp.dma_start(r3(up, 4), upp_c[:, :, col]).then_inc(raw_in[up], 16)
                        sp.dma_start(raw[up][:, 4 * P:6 * P].rearrange("p (k c) -> p k c", c=P),
                                     upa_c[:, :, col]).then_inc(raw_in[up], 16)
                        if j == 0:
                            raws_free(s, i, 1)
                        else:
                            sp.wait_ge(w_ready[0], split_by(s, 0, F_PROJ + i * F_GATE + 2))
                        sp.dma_start(r3(ga, 8), w_gate_c[:, :, col]).then_inc(raw_in[ga], 16)
                        sp.wait_ge(w_ready[up], split_by(s, up, F_PROJ + i * F_GATE + (1 if j == 0 else 2)))
                        sp.dma_start(r3(gb, 8), w_gate_c[:, :, bass.ds(i * 256 + P * j + D, P)]
                                     ).then_inc(raw_in[gb], 16)
                    for j in range(2):
                        sp.wait_ge(w_ready[j], split_by(s, j, F_PROJ + i * F_GATE + 3))
                        sp.dma_start(raw[j][:, :], w_out_r[i * 2 + j]).then_inc(raw_in[j], 16)
                f0 = F_PROJ + GATE_STEPS * F_GATE
                with sp.Fori(0, FFN_STEPS) as i:
                    for j in range(2):
                        col = bass.ds(i * 256 + P * j, P)
                        for k, w in enumerate((fg_c, fu_c)):
                            if j == 0:
                                sp.wait_ge(w_ready[2 + k], s * D_TOTAL + i + (1 + D_PROJ + GATE_STEPS))
                            else:
                                sp.wait_ge(w_ready[k], split_by(s, k, f0 + i * F_FFN + 1))
                            sp.dma_start(r3(k, 8), w[:, :, col]).then_inc(raw_in[k], 16)
                    for j in range(2):
                        sp.wait_ge(w_ready[j], split_by(s, j, f0 + i * F_FFN + 2))
                        sp.dma_start(raw[j][:, :], w_fd_r[i * 2 + j]).then_inc(raw_in[j], 16)

        @block.gpsimd
        def _(pool):
            chain = Chain(pool, w_hi_done)
            for s4 in range(4):
                pool.sem_inc(w_ready[s4], 1)
            nc.gpsimd.memset(zero[:, :], 0.0).then_inc(zeroed, 1)
            pool.wait_ge(zeroed, 1)

            def split(s, r, n_raw, slot, width=D):
                pool.wait_ge(raw_in[r], (s * RAW_TOTAL + n_raw) * 16)
                chain.link(nc.gpsimd.tensor_tensor(w_hi[slot][:, 0:width], raw[r][:, 0:width],
                                                   zero[:, :].broadcast_to([P, width]), ALU.add))
                nc.gpsimd.tensor_tensor(w_lo[slot][:, 0:width], raw[r][:, 0:width],
                                        w_hi[slot][:, 0:width].bitcast(F32), ALU.subtract
                                        ).then_inc(w_ready[slot], 1)

            SPLITS = len(CHUNKS) + 8 * GATE_STEPS + 6 * FFN_STEPS
            with pool.Fori(0, SEQS) as s:
                saved = chain.enter(s, SPLITS)
                last_use = {}
                for c, (slot, what, job) in enumerate(CHUNKS):
                    if slot in last_use:
                        b, n = PLAN.job[last_use[slot]]
                        pool.wait_ge(bank_full[b], filled(s, b, n))
                    else:
                        b, n = ((5, -2), (7, -2), (0, 0), (7, 0))[slot]
                        pool.wait_ge(bank_full[b], filled(s, b, n))
                    last_use[slot] = job
                    split(s, c % 2, c // 2 + 1, slot, 2 * P if what[0] == "maps" else D)
                with pool.Fori(0, GATE_STEPS) as i:
                    inner = chain.enter(i, 8)

                    def gate_use(b, n):
                        pool.wait_ge(bank_full[b], filled(s, b, PLAN.gate0[b] + i * GATE_FILLS + n))

                    r0 = RAW_PROJ + i * 5
                    b, n = PLAN.job["mix", 3]
                    pool.wait_ge(bank_full[b], filled(s, b, n))
                    gate_use(5, -2)
                    split(s, 0, r0 + 2, 0, 6 * P)
                    b, n = PLAN.job["mix", 7]
                    pool.wait_ge(bank_full[b], filled(s, b, n))
                    gate_use(7, -2)
                    split(s, 1, r0 + 1, 1)
                    gate_use(3, 1)
                    split(s, 0, r0 + 3, 0)
                    gate_use(5, 1)
                    split(s, 1, r0 + 3, 1, 6 * P)
                    gate_use(7, 1)
                    split(s, 0, r0 + 4, 0)
                    gate_use(3, 2)
                    split(s, 1, r0 + 4, 1)
                    gate_use(0, 0)
                    split(s, 0, r0 + 5, 2)
                    gate_use(7, 0)
                    split(s, 1, r0 + 5, 3)
                    chain.leave(inner, GATE_STEPS, 8)
                with pool.Fori(0, FFN_STEPS) as i:
                    inner = chain.enter(i, 6)

                    def ffn_use(b, n):
                        pool.wait_ge(bank_full[b], filled(s, b, PLAN.ffn0[b] + i * FFN_FILLS + n))

                    r0 = RAW_PROJ + GATE_STEPS * 5 + i * 3
                    ffn_use(5, -2)
                    split(s, 0, r0 + 1, 0)
                    ffn_use(7, -2)
                    split(s, 1, r0 + 1, 1)
                    ffn_use(1, 1)
                    split(s, 0, r0 + 2, 0)
                    ffn_use(3, 1)
                    split(s, 1, r0 + 2, 1)
                    ffn_use(0, 0)
                    split(s, 0, r0 + 3, 2)
                    ffn_use(7, 0)
                    split(s, 1, r0 + 3, 3)
                    chain.leave(inner, FFN_STEPS, 6)
                chain.leave(saved, SEQS, SPLITS)

        @block.tensor
        def _(pe):
            for b in range(8):
                pe.sem_inc(bank_full[b], CREDIT["bank_full"])
            pe.wait_ge(const_in, 16 * 6)

            def col_job(bank, slot, half, ks, first, last, rhs=(h_hi, h_lo), w0=0):
                o = ps[:, bank, :]
                for k in ks:
                    wh = w_hi[slot][:, (w0 + k) * P:(w0 + k + 1) * P]
                    wl = w_lo[slot][:, (w0 + k) * P:(w0 + k + 1) * P]
                    rh, rl = (r[:, k, half * H2:(half + 1) * H2] for r in rhs)
                    nc.tensor.matmul(o, wh, rh, start=(k == first), stop=False)
                    nc.tensor.matmul(o, wh, rl, start=False, stop=False)
                    ins = nc.tensor.matmul(o, wl, rh, start=False, stop=(k == last))
                if ks[-1] == last:
                    ins.then_inc(bank_full[bank], 1)

            def perm(hx, k, g, first):
                d, n = DIL[g], T // DIL[g]
                return hx[:, k, :].rearrange("p (i r) -> p r i", r=d)[:, first // n, first % n:first % n + P]

            def v_job(bank, g, v, ks):
                o = ps[:, bank, 0:256]
                first = v_tokens(g)[v]
                for k in ks:
                    slot, kk = 2 + k // 4, k % 4
                    rh = w_hi[slot][:, kk * 256:(kk + 1) * 256]
                    rl = w_lo[slot][:, kk * 256:(kk + 1) * 256]
                    lh, ll = perm(h_hi, k, g, first), perm(h_lo, k, g, first)
                    nc.tensor.matmul(o, lh, rh, start=(k == 0), stop=False)
                    nc.tensor.matmul(o, lh, rl, start=False, stop=False)
                    ins = nc.tensor.matmul(o, ll, rh, start=False, stop=(k == KD - 1))
                if ks[-1] == KD - 1:
                    ins.then_inc(bank_full[bank], 1)

            def proj_steps(s, job, ks):
                j, bank = job[-1], PLAN.job[job][0]
                if ks[0] == 0:
                    reader, n = PLAN.before[job]
                    pe.wait_ge(sems[reader], due(reader, s, n))
                if job[0] == "u":
                    tile, half, chunks = j // 2, j % 2, 2 * GROUPS
                elif j < 8:
                    (tile, half), chunks = order(job[1], j), 2 * job[1]
                else:
                    if ks[0] == 0:
                        pe.wait_ge(w_ready[2], split_by(s, 2, job[1] + 1))
                        pe.wait_ge(w_ready[3], split_by(s, 3, job[1] + 1))
                    v_job(bank, job[1], j - 8, ks)
                    return
                if ks[0] == 0 and half == 0:
                    pe.wait_ge(w_ready[tile % 2], split_by(s, tile % 2, chunks + tile // 2 + 1))
                if job in (("proj", 0, 0), ("proj", 0, 2)) and ks[0] == 0:
                    pe.wait_ge(h_ready, due("h_ready", s, 8 * (half + 1)))
                col_job(bank, tile % 2, half, ks, 0, KD - 1)

            def projections(s, part):
                for job, k in PARTS[part]:
                    proj_steps(s, job, [k])

            def norm_transposes(s, which, tiles):
                for t in tiles:
                    pe.wait_ge(xn_ready, due("xn_ready", s, 8 * (which - 1) + t + 1))
                    for half in range(2):
                        b = PLAN.job[f"n{which}", t, half][0]
                        reader, n = PLAN.before[f"n{which}", t, half]
                        pe.wait_ge(sems[reader], due(reader, s, n))
                        for k in range(4):
                            c = (4 * half + k) * P
                            ins = nc.tensor.transpose(ps[:, b, k * P:(k + 1) * P], xn[:, t % 2, c:c + P],
                                                      ident_sb[:, :])
                        ins.then_inc(bank_full[b], 1)

            def scores(s, unit):
                g, u = unit // UNITS, unit % UNITS
                pair, b = u // TT, u % TT
                lo, wid, _, _ = window(g, b)
                if u == 0:
                    pe.wait_ge(qk_ready, due("qk_ready", s, 8 * (g + 1)))
                for h in range(2):
                    bank = PLAN.job["s", unit, h][0]
                    reader, n = PLAN.before["s", unit, h]
                    pe.wait_ge(sems[reader], due(reader, s, n))
                    rows = slice(HEAD * h, HEAD * h + HEAD)
                    nc.tensor.matmul(ps[:, bank, 0:wid], qk[g % 2][rows, pair, b * P:(b + 1) * P],
                                     qk[g % 2][rows, 2 + pair, lo:lo + wid], start=True, stop=True
                                     ).then_inc(bank_full[bank], 1)

            def prob_transposes(s, unit):
                g, u = unit // UNITS, unit % UNITS
                wid = window(g, u % TT)[1]
                pe.wait_ge(p_ready, due("p_ready", s, unit + 1))
                bank = PLAN.job["pt", unit][0]
                reader, n = PLAN.before["pt", unit]
                pe.wait_ge(sems[reader], due(reader, s, n))
                n = 0
                for h in range(2):
                    for c in range(wid // P):
                        ins = nc.tensor.transpose(ps[:, bank, n * P:(n + 1) * P],
                                                  prob[:, u % 2, h, c * P:(c + 1) * P], ident_sb[:, :])
                        n += 1
                ins.then_inc(bank_full[bank], 1)

            def prob_v(s, unit):
                g, u = unit // UNITS, unit % UNITS
                pair = u // TT
                tiles = window(g, u % TT)[2]
                if u == 0:
                    pe.wait_ge(v_ready, due("v_ready", s, sum(N_V[:g + 1])))
                pe.wait_ge(pt_ready, due("pt_ready", s, unit + 1))
                bank = PLAN.job["o", unit][0]
                reader, n = PLAN.before["o", unit]
                pe.wait_ge(sems[reader], due(reader, s, n))
                n = 0
                for h in range(2):
                    e = (2 * pair + h) * HEAD
                    for c, v in enumerate(tiles):
                        ins = nc.tensor.matmul(ps[:, bank, h * HEAD:(h + 1) * HEAD], probT[:, n, :],
                                               V[g % 2][:, v, e:e + HEAD], start=(c == 0),
                                               stop=(c == len(tiles) - 1))
                        n += 1
                ins.then_inc(bank_full[bank], 1)

            def row_step(s, n_w, n_y, n_x, reader):
                for rnd in range(2):
                    for j in range(2):
                        if rnd == 0:
                            pe.wait_ge(w_ready[2 + j], split_by(s, 2 + j, n_w))
                            pe.wait_ge(y_ready, due("y_ready", s, n_y + 2 * j + 2))
                        for b in range(8):
                            t, n = (8 * rnd + b) // 2, b % 2
                            if j == 0 and rnd == 0:
                                pe.wait_ge(sems[reader[b][0]], due(reader[b][0], s, reader[b][1]))
                            elif j == 0:
                                pe.wait_ge(x_added, due("x_added", s, n_x + b + 1))
                            o = ps[:, b, :]
                            tok, col = slice(t * P, (t + 1) * P), slice(n * H2, (n + 1) * H2)
                            nc.tensor.matmul(o, y_hi[j][:, tok], w_hi[2 + j][:, col], start=(j == 0), stop=False)
                            nc.tensor.matmul(o, y_hi[j][:, tok], w_lo[2 + j][:, col], start=False, stop=False)
                            ins = nc.tensor.matmul(o, y_lo[j][:, tok], w_hi[2 + j][:, col],
                                                   start=False, stop=(j == 1))
                            if j == 1:
                                ins.then_inc(bank_full[b], 1)

            with pe.Fori(0, SEQS) as s:
                norm_transposes(s, 1, range(5))
                for n, t in enumerate((5, 6, 7)):
                    proj_steps(s, ("proj", 0, n // 2), range(4 * (n % 2), 4 * (n % 2) + 4))
                    norm_transposes(s, 1, [t])
                proj_steps(s, ("proj", 0, 1), range(4, 8))
                for j in range(2, 8 + N_V[0]):
                    proj_steps(s, ("proj", 0, j), range(KD))
                for unit in range(GROUPS * UNITS + 1):
                    busy = unit < GROUPS * UNITS
                    if busy:
                        scores(s, unit)
                        projections(s, 3 * unit)
                    if unit:
                        prob_transposes(s, unit - 1)
                    if busy:
                        projections(s, 3 * unit + 1)
                    if unit:
                        prob_v(s, unit - 1)
                    if busy:
                        projections(s, 3 * unit + 2)
                for j in range(8):
                    g, half = j // 2, j % 2
                    b = PLAN.job["mix", j][0]
                    reader, n = PLAN.before["mix", j]
                    pe.wait_ge(sems[reader], due(reader, s, n))
                    if half == 0:
                        pe.wait_ge(pool_ready, due("pool_ready", s, g + 1))
                        if g % 2 == 0:
                            pe.wait_ge(w_ready[g // 2], split_by(s, g // 2, F_PROJ))
                    o, m = ps[:, b, :], slice((g % 2) * P, (g % 2 + 1) * P)
                    tok = slice(half * H2, (half + 1) * H2)
                    nc.tensor.matmul(o, w_hi[g // 2][:, m], pool_hi[:, tok], start=True, stop=False)
                    nc.tensor.matmul(o, w_hi[g // 2][:, m], pool_lo[:, tok], start=False, stop=False)
                    nc.tensor.matmul(o, w_lo[g // 2][:, m], pool_hi[:, tok], start=False, stop=True
                                     ).then_inc(bank_full[b], 1)
                for t in range(TT):
                    pe.wait_ge(mtok_ready, due("mtok_ready", s, t + 1))
                    for pair in range(2):
                        job = ("mt", 2 * (t // 4) + pair)
                        b = PLAN.job[job][0]
                        if t % 4 == 0:
                            reader, n = PLAN.before[job]
                            pe.wait_ge(sems[reader], due(reader, s, n))
                        ins = nc.tensor.transpose(ps[:, b, (t % 4) * P:(t % 4 + 1) * P],
                                                  mtok[:, t, pair * P:(pair + 1) * P], ident_sb[:, :])
                        if t % 4 == 3:
                            ins.then_inc(bank_full[b], 1)
                with pe.Fori(0, GATE_STEPS) as i:
                    pe.wait_ge(mixed_ready, due("mixed_ready", s, 8))
                    pe.wait_ge(mT_ready, due("mT_ready", s, 4))
                    for j in range(2):
                        slots = [(3 * j + c) % 2 for c in range(3)]
                        counts = [(1, 1, 2), (2, 3, 3)][j]
                        f = i * 2 + (j - 1)

                        def bank_read(b, name, n):
                            if j == 0:
                                pe.wait_ge(x_added, due("x_added", s, i * 16 + (b + 1 - 8)))
                            else:
                                pe.wait_ge(sems[name], due(name, s, n))

                        for c in range(3):
                            pe.wait_ge(w_ready[slots[c]], split_by(s, slots[c], i * F_GATE + (F_PROJ + counts[c])))
                            for half in range(2):
                                if c == 0:
                                    bank_read(half, "a_read", f * 2 + (half + 1))
                                    col_job(half, slots[0], half, range(4), 0, 3, (mix_hi, mix_lo))
                                else:
                                    b = 2 + 2 * c + half
                                    bank_read(b, "sig_ready", f * 4 + (2 * (c - 1) + half + 1))
                                    col_job(b, slots[c], half, range(KD), 0, KD - 1)
                            for half in range(2):
                                if c == 0:
                                    bank_read(2 + half, "b_read", f * 2 + (half + 1))
                                    col_job(2 + half, slots[0], half, range(2), 0, 1, (m_hi, m_lo), 4)
                    last = i * 2 + 1
                    reader = ([(name, last * 2 + (half + 1)) for name in ("a_read", "b_read") for half in range(2)]
                              + [("sig_ready", last * 4 + (n + 1)) for n in range(4)])
                    row_step(s, i + (D_PROJ + 1), i * 4, i * 16, reader)
                norm_transposes(s, 2, range(TT))
                with pe.Fori(0, FFN_STEPS) as i:
                    pe.wait_ge(htmp_ready, due("htmp_ready", s, 32))
                    for j in range(2):
                        for c in range(2):
                            pe.wait_ge(w_ready[c], split_by(s, c, i * F_FFN + (F_PROJ + GATE_STEPS * F_GATE + j + 1)))
                            for half in range(2):
                                b = 4 * j + 2 * c + half
                                pe.wait_ge(x_added, due("x_added", s, i * 16 + (16 * GATE_STEPS + b + 1 - 8)))
                                if j == 0 and c == 0:
                                    pe.wait_ge(h_ready, due("h_ready", s, 16 + 8 * (half + 1)))
                                col_job(b, c, half, range(KD), 0, KD - 1)
                    reader = [("sig_ready" if (b // 2) % 2 == 0 else "y_sum",
                               (32 if (b // 2) % 2 == 0 else 16) + 2 * (b // 4) + b % 2 + 1 + i * 4) for b in range(8)]
                    row_step(s, i + (D_PROJ + GATE_STEPS + 1), i * 4 + 16, i * 16 + 16 * GATE_STEPS, reader)

        @block.scalar
        def _(act):
            act.sem_inc(p_ready, CREDIT["p_ready"])
            for n in range(2):
                act.sem_inc(out_stored[n], CREDIT[f"out_stored{n}"])
            for dst, src in ((ident_sb[:, :], ident), (g_mix[:, :], norm_mix), (g_ffn[:, :], norm_ffn),
                             (p_scale[:, :], pool_scale), (b_g[:, :], b_gate),
                             (edge_sb[:, :, :], edge)):
                act.dma_start(dst, src).then_inc(const_in, 16)
            act.wait_ge(eps_set, 1)
            act.wait_ge(const_in, 16 * 6)

            def stats(s, n, t):
                nc.scalar.activation(squares[:, :], X[:, t, :], ACT.Square, accum_out=ss[:, t % 2:t % 2 + 1]
                                     ).then_inc(ss_ready, 1)
                act.wait_ge(ss_ready, due("ss_ready", s, n))
                nc.scalar.activation(std[:, t % 2:t % 2 + 1], ss[:, t % 2:t % 2 + 1], ACT.Sqrt,
                                     bias=eps[:, :], scale=1.0 / D).then_inc(std_ready, 1)

            def round_h(s, which, t):
                for half in range(2):
                    act.wait_ge(htmp_ready, due("htmp_ready", s, 16 * (which - 1) + 2 * t + half + 1))
                    nc.scalar.copy(h_hi[:, 4 * half:4 * half + 4, t * P:(t + 1) * P], n_tmp[:, half, :, :]
                                   ).then_inc(hhi_ready, 1)

            def evict_v(s, g, v):
                b, n = PLAN.job["proj", g, 8 + v]
                act.wait_ge(bank_full[b], filled(s, b, n))
                nc.scalar.copy(V[g % 2][:, v, :], ps[:, b, 0:256]).then_inc(v_ready, 1)

            def exp_unit(s, unit):
                u = unit
                wid = window(unit // UNITS, unit % TT)[1]
                act.wait_ge(negmax_ready, due("negmax_ready", s, unit + 1))
                for h in range(2):
                    ins = nc.scalar.activation(prob[:, u % 2, h, 0:wid], masked[:, h, 0:wid], ACT.Exp,
                                               bias=o_st[:, u % 4, 2 * HEAD + h:2 * HEAD + h + 1],
                                               scale=HEAD ** -0.5,
                                               accum_out=o_st[:, u % 4, 2 * HEAD + 2 + h:2 * HEAD + 3 + h])
                ins.then_inc(p_ready, 1)

            def evict_probs(s, unit):
                wid = window(unit // UNITS, unit % TT)[1]
                b, n = PLAN.job["pt", unit]
                act.wait_ge(bank_full[b], filled(s, b, n))
                nc.scalar.copy(probT[:, 0:2 * wid // P, :],
                               ps[:, b, 0:2 * wid].rearrange("p (n q) -> p n q", q=P)
                               ).then_inc(pt_ready, 1)

            def evict_unit(s, unit):
                g, u = unit // UNITS, unit % UNITS
                b, n = PLAN.job["o", unit]
                act.wait_ge(bank_full[b], filled(s, b, n))
                nc.scalar.copy(o_st[:, u % 4, 0:2 * HEAD], ps[:, b, 0:2 * HEAD]).then_inc(o_ready, 1)
                act.wait_ge(o_ready, due("o_ready", s, unit + 1))
                pair, qb = u // TT, u % TT
                by_res = scratch[2 * g + pair].rearrange("(i r) c -> r i c", r=DIL[g])
                n = T // DIL[g] // P
                act.dma_start(by_res[qb // n, (qb % n) * P:(qb % n + 1) * P, :], o_st[:, u % 4, :]
                              ).then_inc(o_stored[u % 4], 16)

            def load_rec(s, t):
                act.dma_start(rec[:, t % 4, :, :], scratch[:, t * P:(t + 1) * P, :].rearrange("q t c -> t q c")
                              ).then_inc(rec_in[t % 4], 16)

            with act.Fori(0, SEQS) as s:
                for t in range(TT):
                    act.dma_start(X[:, t, :], x_t[s, t]).then_inc(x_in[t], 16)
                for dst, src in ((rope_sb[:, :, :], rope), (masks_sb[:, :, :], masks), (diag_sb[:, :], diag)):
                    act.dma_start(dst, src).then_inc(tab_in, 16)
                for t in range(TT + 1):
                    if t < TT:
                        act.wait_ge(x_in[t], due(f"x_in{t}", s, 1))
                        stats(s, t + 1, t)
                    if t:
                        round_h(s, 1, t - 1)
                for n in range(2):
                    act.wait_ge(out_stored[n], due(f"out_stored{n}", s, 0))
                for v in range(N_V[0]):
                    evict_v(s, 0, v)
                for unit in range(GROUPS * UNITS + 1):
                    if unit:
                        evict_probs(s, unit - 1)
                    if unit < GROUPS * UNITS:
                        exp_unit(s, unit)
                    if unit:
                        evict_unit(s, unit - 1)
                        for job in done(3 * unit - 1, 3 * unit + 1):
                            if job[0] == "u":
                                b, n = PLAN.job[job]
                                j = job[1]
                                act.wait_ge(bank_full[b], filled(s, b, n))
                                nc.scalar.copy(U[:, j // 2, (j % 2) * H2:(j % 2 + 1) * H2], ps[:, b, :]
                                               ).then_inc(u_ready, 1)
                            elif job[2] >= 8:
                                evict_v(s, job[1], job[2] - 8)
                for g in range(POOL_GROUPS):
                    act.wait_ge(pooled_ready, due("pooled_ready", s, g + 1))
                    nc.scalar.copy(pool_hi[:, :], pooled[:, :]).then_inc(pool_hi_ready, 1)
                for n in range(4):
                    act.wait_ge(o_stored[n], due(f"o_stored{n}", s, 12))
                for t in range(4):
                    load_rec(s, t)
                for t in range(TT):
                    act.wait_ge(diff_ready, due("diff_ready", s, t + 1))
                    nc.scalar.activation(e3[:, :, :], d3[:, :, :], ACT.Exp).then_inc(weight_ready, 1)
                    if t < 4:
                        act.wait_ge(mtok_ready, due("mtok_ready", s, t + 1))
                        load_rec(s, t + 4)
                for j in range(4):
                    b, n = PLAN.job["mt", j]
                    act.wait_ge(bank_full[b], filled(s, b, n))
                    nc.scalar.copy(m_hi[:, j % 2, (j // 2) * H2:(j // 2 + 1) * H2], ps[:, b, :]
                                   ).then_inc(mhi_ready, 1)
                for t in range(TT):
                    act.dma_start(X[:, t, :], x_t[s, t]).then_inc(x_in[t], 16)
                with act.Fori(0, GATE_STEPS) as i:
                    for j in range(2):
                        f = i * 2 + j
                        nc.scalar.copy(b_now[:, :], b_g[:, :].rearrange("p (g f) -> p f g", g=2)[:, bass.ds(f, 1), :]
                                       .rearrange("p a g -> p (a g)")).then_inc(bias_ready, 1)
                        act.wait_ge(bias_ready, due("bias_ready", s, f + 1))
                        for half in range(2):
                            act.wait_ge(bank_full[4 + half], filled(s, 4 + half, i * GATE_FILLS + (PLAN.gate0[4 + half] + j + 1)))
                            act.wait_ge(y_ready, due("y_ready", s, f * 2 + (half - 1)))
                            nc.scalar.activation(act_t[:, half, :], ps[:, 4 + half, :], ACT.Sigmoid,
                                                 bias=b_now[:, 0:1]).then_inc(sig_ready, 1)
                        for half in range(2):
                            act.wait_ge(bank_full[6 + half], filled(s, 6 + half, i * GATE_FILLS + (PLAN.gate0[6 + half] + j + 1)))
                            act.wait_ge(y_sum, due("y_sum", s, f * 2 + half))
                            nc.scalar.activation(act_t[:, 2, :], ps[:, 6 + half, :], ACT.Sigmoid,
                                                 bias=b_now[:, 1:2]).then_inc(sig_ready, 1)
                            act.wait_ge(y_sum, due("y_sum", s, f * 2 + (half + 1)))
                            nc.scalar.copy(y_hi[j][:, half * H2:(half + 1) * H2], act_t[:, half, :]
                                           ).then_inc(yhi_ready, 1)
                for t in range(TT + 1):
                    if t < TT:
                        act.wait_ge(x_added, due("x_added", s, 16 * GATE_STEPS - 16 + 2 * (t + 1)))
                        if t == 0:
                            act.dma_start(g_fin[:, :], norm_final.partition_broadcast(P)
                                          ).then_inc(gfin_in, 16)
                        stats(s, TT + t + 1, t)
                    if t:
                        round_h(s, 2, t - 1)
                with act.Fori(0, FFN_STEPS) as i:
                    for j in range(2):
                        n = i * 4 + (16 + 2 * j)
                        for half in range(2):
                            act.wait_ge(bank_full[4 * j + half], filled(s, 4 * j + half, i * FFN_FILLS + (PLAN.ffn0[4 * j + half] + 1)))
                            act.wait_ge(y_ready, due("y_ready", s, n + (half - 1)))
                            nc.scalar.activation(act_t[:, half, :], ps[:, 4 * j + half, :], ACT.Silu
                                                 ).then_inc(sig_ready, 1)
                        for half in range(2):
                            act.wait_ge(y_sum, due("y_sum", s, n + (half + 1)))
                            nc.scalar.copy(y_hi[j][:, half * H2:(half + 1) * H2], act_t[:, half, :]
                                           ).then_inc(yhi_ready, 1)
                for t in range(TT + 1):
                    if t < TT:
                        act.wait_ge(x_added, due("x_added", s, PER_SEQ["x_added"] - 16 + 2 * (t + 1)))
                        stats(s, 2 * TT + t + 1, t)
                    if t:
                        act.wait_ge(fin_ready, due("fin_ready", s, t))
                        act.dma_start(out_t[s, t - 1], fin[:, (t - 1) % 2, :]).then_inc(out_stored[(t - 1) % 2], 16)
            for n in range(2):
                act.wait_ge(out_stored[n], due(f"out_stored{n}", SEQS, 0))

        @block.vector
        def _(dve):
            dve.sem_inc(y_sum, CREDIT["y_sum"])
            dve.sem_inc(y_ready, CREDIT["y_ready"])
            dve.sem_inc(x_added, CREDIT["x_added"])
            nc.vector.memset(eps[:, :], EPS).then_inc(eps_set, 1)
            dve.wait_ge(const_in, 16 * 6)
            chain = Chain(dve, dve_chain)
            V_ = nc.vector

            def rsqrt(s, n, t):
                dve.wait_ge(std_ready, due("std_ready", s, n))
                chain.link(V_.reciprocal(rstd[:, t % 2:t % 2 + 1], std[:, t % 2:t % 2 + 1]))

            def norm(s, which, gain):
                for t in range(TT + 1):
                    if t < TT:
                        rsqrt(s, 8 * (which - 1) + t + 1, t)
                        V_.tensor_scalar(xn[:, t % 2, :], X[:, t, :], rstd[:, t % 2:t % 2 + 1], None, ALU.mult
                                         ).then_inc(xn_ready, 1)
                    if t:
                        v = t - 1
                        for half in range(2):
                            if v:
                                dve.wait_ge(h_ready, due("h_ready", s, 16 * (which - 1) + 2 * v + half - 1))
                            b, n = PLAN.job[f"n{which}", v, half]
                            dve.wait_ge(bank_full[b], filled(s, b, n))
                            V_.tensor_tensor(n_tmp[:, half, :, :], ps[:, b, :].rearrange("p (k q) -> p k q", q=P),
                                             gain[:, 4 * half:4 * half + 4].unsqueeze(2).broadcast_to([P, 4, P]),
                                             ALU.mult).then_inc(htmp_ready, 1)
                        for half in range(2):
                            dve.wait_ge(hhi_ready, due("hhi_ready", s, 16 * (which - 1) + 2 * v + half + 1))
                            at_h = (slice(None), slice(4 * half, 4 * half + 4), slice(v * P, (v + 1) * P))
                            V_.tensor_tensor(h_lo[at_h], n_tmp[:, half, :, :], h_hi[at_h].bitcast(F32),
                                             ALU.subtract).then_inc(h_ready, 1)

            partner = [i + 8 if i < 8 else i - 8 if i < 16 else i for i in range(32)]

            def rope_job(s, g, j):
                tile, half = order(g, j)
                if j:
                    dve.wait_ge(qk_ready, due("qk_ready", s, 8 * g + j))
                b, n = PLAN.job["proj", g, j]
                dve.wait_ge(bank_full[b], filled(s, b, n))
                tok = slice(half * H2, (half + 1) * H2)
                V_.tensor_tensor(r_c[:, :], ps[:, b, :], rope_sb[:, 0, tok], ALU.mult)
                chain.link(V_.stream_shuffle(r_sh[:, :], ps[:, b, :], partner))
                V_.tensor_tensor(r_s[:, :], r_sh[:, :], rope_sb[:, 1, tok], ALU.mult).then_inc(rope_read, 1)
                dve.wait_ge(rope_read, due("rope_read", s, 8 * g + j + 1))
                d = DIL[g]
                n = H2 // d
                V_.tensor_tensor(qk[g % 2][:, tile, :].rearrange("p (r i) -> p r i", r=d)[:, :, half * n:(half + 1) * n],
                                 r_c[:, :].rearrange("p (i r) -> p r i", r=d),
                                 r_s[:, :].rearrange("p (i r) -> p r i", r=d), ALU.add
                                 ).then_inc(qk_ready, 1)

            def softmax_unit(s, unit):
                _, wid, _, m = window(unit // UNITS, unit % TT)
                for h in range(2):
                    b, n = PLAN.job["s", unit, h]
                    dve.wait_ge(bank_full[b], filled(s, b, n))
                n = unit
                dve.wait_ge(p_ready, due("p_ready", s, n))
                mask = diag_sb[:, 0:wid] if m == 3 else masks_sb[:, m, 0:wid]
                V_.tensor_tensor(masked[:, :, 0:wid], ps[:, 4:6, 0:wid],
                                 mask.unsqueeze(1).broadcast_to([P, 2, wid]), ALU.add
                                 ).then_inc(s_read, 1)
                dve.wait_ge(s_read, due("s_read", s, n + 1))
                chain.link(V_.reduce_max(mx[:, :], masked[:, :, 0:wid], AX_X))
                if n >= 4:
                    dve.wait_ge(o_stored[n % 4], due(f"o_stored{n % 4}", s, n // 4))
                V_.tensor_scalar(o_st[:, n % 4, 2 * HEAD:2 * HEAD + 2], mx[:, :], -HEAD ** -0.5, None, ALU.mult
                                 ).then_inc(negmax_ready, 1)

            def evict_mix(s, g):
                for half in range(2):
                    b, n = PLAN.job["mix", 2 * g + half]
                    dve.wait_ge(bank_full[b], filled(s, b, n))
                    tok = slice(half * H2, (half + 1) * H2)
                    chain.link(V_.tensor_scalar(mix_hi[:, g, tok], ps[:, b, :], p_scale[:, g:g + 1], None, ALU.mult))
                    V_.scalar_tensor_tensor(out=mix_lo[:, g, tok], in0=ps[:, b, :], scalar=p_scale[:, g:g + 1],
                                            in1=mix_hi[:, g, tok].bitcast(F32), op0=ALU.mult, op1=ALU.subtract
                                            ).then_inc(mixed_ready, 1)

            def pool_windows(s, g):
                w = 2 << g
                dve.wait_ge(u_ready, due("u_ready", s, 2 * (g + 1)))
                V_.memset(pw0[:, 0:8], 0.0)
                V_.memset(pw0[:, 1032:1040], 0.0)
                chain.link(V_.tensor_copy(pw0[:, 8:1032], U[:, g, :]))
                cur, nxt, n = pw0, pw1, 1040
                for k in range(g + 1):
                    n -= 1 << k
                    chain.link(V_.tensor_tensor(nxt[:, 0:n], cur[:, 0:n], cur[:, (1 << k):n + (1 << k)], ALU.add))
                    cur, nxt = nxt, cur
                a = 8 - w // 2
                V_.tensor_tensor(cur[:, a:a + 8], cur[:, a:a + 8], edge_sb[:, g, 0:8], ALU.mult)
                chain.link(V_.tensor_tensor(cur[:, a + 1016:a + 1024], cur[:, a + 1016:a + 1024],
                                            edge_sb[:, g, 8:16], ALU.mult))
                if g:
                    evict_mix(s, g - 1)
                V_.scalar_tensor_tensor(out=pooled[:, :], in0=cur[:, a:a + T], scalar=1.0 / w, in1=U[:, g, :],
                                        op0=ALU.mult, op1=ALU.subtract).then_inc(pooled_ready, 1)
                dve.wait_ge(pool_hi_ready, due("pool_hi_ready", s, g + 1))
                V_.tensor_tensor(pool_lo[:, :], pooled[:, :], pool_hi[:, :].bitcast(F32), ALU.subtract
                                 ).then_inc(pool_ready, 1)

            def merge(s, t):
                dve.wait_ge(rec_in[t % 4], due(f"rec_in{t % 4}", s, t // 4 + 1))
                r = rec[:, t % 4, :, :]

                def heads(a):
                    return a.rearrange("p (q h) -> p q h", q=2)

                neg = [r[:, 2 * g:2 * g + 2, 2 * HEAD:2 * HEAD + 2] for g in range(GROUPS)]
                dens = [r[:, 2 * g:2 * g + 2, 2 * HEAD + 2:2 * HEAD + 4] for g in range(GROUPS)]
                chain.link(V_.tensor_tensor(heads(mn[:, :]), neg[0], neg[1], ALU.min))
                chain.link(V_.tensor_tensor(heads(mn[:, :]), heads(mn[:, :]), neg[2], ALU.min))
                for g in range(GROUPS):
                    ins = V_.tensor_tensor(heads(d3[:, g, :]), heads(mn[:, :]), neg[g], ALU.subtract)
                ins.then_inc(diff_ready, 1)
                dve.wait_ge(weight_ready, due("weight_ready", s, t + 1))
                for g in range(GROUPS):
                    ins = V_.tensor_tensor(heads(wd[:, g, :]), heads(e3[:, g, :]), dens[g], ALU.mult)
                chain.link(ins)
                chain.link(V_.tensor_tensor(den[:, :], wd[:, 0, :], wd[:, 1, :], ALU.add))
                chain.link(V_.tensor_tensor(den[:, :], den[:, :], wd[:, 2, :], ALU.add))
                chain.link(V_.reciprocal(rden[:, :], den[:, :]))
                chain.link(V_.tensor_tensor(coef[:, :, :], e3[:, :, :], rden[:, :].unsqueeze(1).broadcast_to([P, 3, 4]),
                                            ALU.mult))
                o = [[r[:, 2 * g + q, 0:2 * HEAD].rearrange("p (h e) -> p h e", h=2) for q in range(2)]
                     for g in range(GROUPS)]
                for g in range(GROUPS):
                    for q in range(2):
                        ins = V_.tensor_tensor(o[g][q], o[g][q],
                                               coef[:, g, 2 * q:2 * q + 2].unsqueeze(2).broadcast_to([P, 2, HEAD]),
                                               ALU.mult)
                chain.link(ins)
                chain.link(V_.tensor_tensor(r[:, 0:2, 0:2 * HEAD], r[:, 0:2, 0:2 * HEAD], r[:, 2:4, 0:2 * HEAD],
                                            ALU.add))
                V_.tensor_tensor(mtok[:, t, :].rearrange("p (q c) -> p q c", q=2), r[:, 0:2, 0:2 * HEAD],
                                 r[:, 4:6, 0:2 * HEAD], ALU.add).then_inc(mtok_ready, 1)

            def add_rows(s, i, fills0, fills_step, first):
                for idx in range(16):
                    b, t, n = idx % 8, idx // 2, idx % 2
                    dve.wait_ge(bank_full[b], filled(s, b, i * fills_step + (fills0[b] + first + idx // 8 + 1)))
                    xs = X[:, t, n * H2:(n + 1) * H2]
                    V_.tensor_tensor(xs, xs, ps[:, b, :], ALU.add).then_inc(x_added, 1)

            def y_low(s, j, half, n):
                dve.wait_ge(yhi_ready, due("yhi_ready", s, n))
                tok = slice(half * H2, (half + 1) * H2)
                V_.tensor_tensor(y_lo[j][:, tok], act_t[:, half, :], y_hi[j][:, tok].bitcast(F32), ALU.subtract
                                 ).then_inc(y_ready, 1)

            with dve.Fori(0, SEQS) as s:
                saved = chain.enter(s, DVE_STEPS)
                norm(s, 1, g_mix)
                dve.wait_ge(tab_in, due("tab_in", s, 3))
                for j in range(8):
                    rope_job(s, 0, j)
                for unit in range(GROUPS * UNITS):
                    softmax_unit(s, unit)
                    for job in done(3 * unit - 3, 3 * unit - 1):
                        if job[0] == "proj" and job[2] < 8:
                            rope_job(s, job[1], job[2])
                for g in range(POOL_GROUPS):
                    pool_windows(s, g)
                evict_mix(s, POOL_GROUPS - 1)
                for t in range(TT):
                    merge(s, t)
                for j in range(4):
                    dve.wait_ge(mhi_ready, due("mhi_ready", s, j + 1))
                    tok = slice((j // 2) * H2, (j // 2 + 1) * H2)
                    V_.tensor_tensor(m_lo[:, j % 2, tok], ps[:, 4 + j, :], m_hi[:, j % 2, tok].bitcast(F32),
                                     ALU.subtract).then_inc(mT_ready, 1)
                with dve.Fori(0, GATE_STEPS) as i:
                    for j in range(2):
                        f = i * 2 + j
                        for half in range(2):
                            dve.wait_ge(sig_ready, due("sig_ready", s, f * 4 + (half + 1)))
                            a = act_t[:, half, :]
                            V_.tensor_tensor(a, a, ps[:, half, :], ALU.mult).then_inc(a_read, 1)
                        for half in range(2):
                            dve.wait_ge(sig_ready, due("sig_ready", s, f * 4 + (half + 3)))
                            c = act_t[:, 2, :]
                            V_.tensor_tensor(c, c, ps[:, 2 + half, :], ALU.mult).then_inc(b_read, 1)
                            dve.wait_ge(b_read, due("b_read", s, f * 2 + (half + 1)))
                            a = act_t[:, half, :]
                            V_.tensor_tensor(a, a, c, ALU.add).then_inc(y_sum, 1)
                            y_low(s, j, half, f * 2 + (half + 1))
                    for t in range(TT):
                        dve.wait_ge(x_in[t], due(f"x_in{t}", s, 2))
                    add_rows(s, i, PLAN.gate0, GATE_FILLS, 2)
                norm(s, 2, g_ffn)
                with dve.Fori(0, FFN_STEPS) as i:
                    for j in range(2):
                        for half in range(2):
                            b = 4 * j + 2 + half
                            dve.wait_ge(sig_ready, due("sig_ready", s, i * 4 + (32 + 2 * j + half + 1)))
                            dve.wait_ge(bank_full[b], filled(s, b, i * FFN_FILLS + (PLAN.ffn0[b] + 1)))
                            a = act_t[:, half, :]
                            V_.tensor_tensor(a, a, ps[:, b, :], ALU.mult).then_inc(y_sum, 1)
                        for half in range(2):
                            y_low(s, j, half, i * 4 + (16 + 2 * j + half + 1))
                    add_rows(s, i, PLAN.ffn0, FFN_FILLS, 1)
                dve.wait_ge(gfin_in, due("gfin_in", s, 1))
                for t in range(TT):
                    if t >= 2:
                        dve.wait_ge(out_stored[t % 2], due(f"out_stored{t % 2}", s, t // 2))
                    rsqrt(s, 16 + t + 1, t)
                    V_.scalar_tensor_tensor(out=fin[:, t % 2, :], in0=X[:, t, :], scalar=rstd[:, t % 2:t % 2 + 1],
                                            in1=g_fin[:, :], op0=ALU.mult, op1=ALU.mult
                                            ).then_inc(fin_ready, 1)
                chain.leave(saved, SEQS, DVE_STEPS)


def constants():
    inv = (THETA ** (-np.arange(ROPE_HALF, dtype=np.float32) / ROPE_HALF)).astype(np.float32)
    ang = np.arange(T, dtype=np.float32)[:, None] * inv[None, :]
    cos, sin = np.cos(ang.astype(np.float64)).T, np.sin(ang.astype(np.float64)).T
    rope = np.zeros((P, 2, T), np.float32)
    rope[:, 0] = 1.0
    for h in range(2):
        a, b = HEAD * h, HEAD * h + ROPE_HALF
        rope[a:b, 0], rope[b:b + ROPE_HALF, 0] = cos, cos
        rope[a:b, 1], rope[b:b + ROPE_HALF, 1] = -sin, sin
    q, k = np.arange(P)[:, None], np.arange(256)[None, :]
    masks = np.stack([np.where(np.abs(k - o - q) <= RADIUS, 0.0, -BIG) for o in (64, 0, 128)], 1)
    kk = np.arange(P)[None, :]
    diag = np.where(q % 2 == kk % 2, 0.0, -BIG)
    edge = np.ones((P, POOL_GROUPS, 16), np.float32)
    for g in range(POOL_GROUPS):
        w = 2 << g
        for c in range(16):
            i = c if c < 8 else T - 16 + c
            edge[:, g, c] = w / (min(i + w // 2, T) - max(i - w // 2, 0))
    return rope, masks.astype(np.float32), diag.astype(np.float32), np.eye(P, dtype=np.float32), edge


WEIGHTS = ("w_in", "pool_maps", "w_up_pool", "w_up_attn", "w_gate", "w_out", "w_ffn_gate", "w_ffn_up",
           "w_ffn_down", "norm_mix", "norm_ffn", "norm_final", "pool_scale", "b_gate")
COLUMNS = ("norm_mix", "norm_ffn", "pool_scale", "b_gate")


def kernel(**inputs):
    import concourse.bacc as bacc
    from concourse.bass_utils import run_bass_kernel_spmd as run

    nc = bacc.Bacc("TRN2", target_bir_lowering=False, num_devices=1)
    arrays = {"x": np.concatenate([np.asarray(inputs["x_prompt"]), np.asarray(inputs["x_sample"])])}
    for name in WEIGHTS:
        a = np.asarray(inputs[name])
        a = a if name == "norm_final" else a[0]
        if name in COLUMNS:
            a = a.reshape(-1, P).T
        arrays[name] = np.ascontiguousarray(a)
    args = [nc.dram_tensor(n, a.shape, F32, kind="ExternalInput").ap() for n, a in arrays.items()]
    consts = [nc.inline_tensor(c, n).ap() for c, n in zip(constants(), ("rope", "masks", "diag", "ident", "edge"))]
    scratch = nc.dram_tensor("records", (2 * GROUPS, T, REC), F32, kind="Internal").ap()
    out = nc.dram_tensor("out", (SEQS, T, D), F32, kind="ExternalOutput").ap()
    encoder(nc, *args, *consts, scratch, out)
    r = run(nc, [arrays], core_ids=[0])
    y = r.results[0]["out"]
    return y[0:1], y[1:2]
```

```python
from contextlib import ExitStack

import numpy as np

import concourse.bass as bass
from concourse import mybir

F32 = mybir.dt.float32
F32R = mybir.dt.float32r
ALU = mybir.AluOpType
ACT = mybir.ActivationFunctionType
AX_X = mybir.AxisListType.X

P = 128
SEQS, T, D = 2, 1024, 1024
KD = D // P
TT = T // P
H2 = 512
HEAD, HPG, GROUPS = 64, 4, 3
DIL = (1, 4, 8)
RADIUS = 64
AW = HEAD * HPG * GROUPS
PW = 512
POOL_GROUPS = 4
FF = 2816
FF_TILES = FF // P
EPS = 1e-6
ROPE_HALF, THETA = 8, 500000.0
REC = 2 * HEAD + 4
UNITS = 2 * TT
BIG = 3.0e38

CREDIT = {"bank_full": 3, "w_ready": 1, "p_ready": 1, "y_sum": 1, "y_ready": 2, "x_added": 8,
          "out_stored0": 16, "out_stored1": 16}
N_V = (11, 8, 8)
PER_SEQ = {
    "ss_ready": 24, "std_ready": 24, "xn_ready": 16, "htmp_ready": 32, "hhi_ready": 32, "h_ready": 32,
    "rope_read": 24, "qk_ready": 24, "v_ready": sum(N_V), "s_read": 48, "negmax_ready": 48, "p_ready": 48,
    "pt_ready": 48, "o_ready": 48, "u_ready": 8, "pooled_ready": 4, "pool_hi_ready": 4, "pool_ready": 4,
    "mix_read": 8, "mix_hi_ready": 4, "mixed_ready": 4, "diff_ready": 2, "weight_ready": 2, "merged": 2, "mhi_ready": 4, "mT_ready": 4,
    "a_read": 16, "b_read": 16, "sig_ready": 76, "y_sum": 60, "yhi_ready": 60, "y_ready": 60,
    "x_added": 240, "fin_ready": 8, "bias_ready": 8,
}
DMA_SEMS = {"tab_in": 3, "gfin_in": 1}
DMA_SEMS.update({f"x_in{t}": 2 for t in range(TT)})
DMA_SEMS.update({"rec_in0": 4, "rec_in1": 4})
DMA_SEMS.update({f"o_stored{n}": 12 for n in range(4)})
DMA_SEMS.update({"out_stored0": 4, "out_stored1": 4})
PER_SEQ.update(DMA_SEMS)


def due(name, s, n):
    step = 16 if name in DMA_SEMS else 1
    return s * (PER_SEQ[name] * step) + (CREDIT.get(name, 0) + n * step)


def v_tokens(g):
    if g:
        return [P * j for j in range(TT)]
    return [64 + P * j for j in range(7)] + [0, 128, 768, 896]


def window(g, b):
    if g == 0:
        if b == 0:
            return 0, 256, (7, 8), 1
        if b == TT - 1:
            return T - 256, 256, (9, 10), 2
        return P * b - 64, 256, (b - 1, b), 0
    if g == 1:
        r = b // 2
        return 256 * r, 256, (2 * r, 2 * r + 1), 1 + b % 2
    return P * b, P, (b,), 3


def phase_steps(g):
    if g == GROUPS - 1:
        return [(("u", j), k) for j in reversed(range(8)) for k in range(KD)]
    tiles = [(("proj", g + 1, j), k) for j in range(8) for k in range(KD)]
    values = [(("proj", g + 1, 8 + v), k) for v in range(N_V[g + 1]) for k in range(KD)]
    steps, tiles = tiles[:2 * KD], tiles[2 * KD:]
    for n in range(len(tiles) // 4):
        steps += tiles[4 * n:4 * n + 4] + values[3 * n:3 * n + 3]
    return steps + values[len(tiles) // 4 * 3:]


def cut(g):
    steps = phase_steps(g)
    n_parts = 3 * UNITS if g < GROUPS - 1 else 3 * (UNITS - 2)
    cost = [1 if job[0] == "proj" and job[2] >= 8 else 2 for job, _ in steps]
    total, parts, at_time = sum(cost), [[] for _ in range(3 * UNITS)], 0
    for step, c in zip(steps, cost):
        parts[at_time * n_parts // total].append(step)
        at_time += c
    return parts


PARTS = [p for g in range(GROUPS) for p in cut(g)] + [[], [], []]


def done(first, last):
    return [job for p in PARTS[max(first, 0):last + 1] for job, k in p if k == KD - 1]


LAST = (GROUPS - 1) * UNITS
POOL_DVE = {LAST + 4: [("add", 3, 0, 1)], LAST + 5: [("add", 3, 2, 3)], LAST + 6: [("mean", 3)],
            LAST + 8: [("lo", 3), ("add", 2, 0, 0)], LAST + 9: [("add", 2, 1, 2)], LAST + 10: [("mean", 2)],
            LAST + 11: [("add", 1, 0, 0)], LAST + 12: [("lo", 2), ("add", 1, 1, 1)], LAST + 13: [("mean", 1)],
            LAST + 15: [("lo", 1), ("add", 0, 0, 0)]}
POOL_ACT = {LAST + 7: 3, LAST + 11: 2, LAST + 14: 1}
for _g, _n in ((3, 9), (2, 13), (1, 16)):
    for _h in range(2):
        PARTS[3 * (LAST + _n) + _h].append((("mix", 2 * _g + _h), KD - 1))



class Plan:

    def __init__(self):
        self.fills = [0] * 8
        self.job, self.before = {}, {}
        self.reader = [("x_added", b + 1 - 8) for b in range(8)]
        self.norm(1)
        for j in range(8 + N_V[0]):
            self.proj(0, j)
        for n in range(GROUPS * UNITS + 1):
            if n < GROUPS * UNITS:
                for h in range(2):
                    self.take(("s", n, h), 4 + h, "s_read", n + 1)
            if n:
                self.take(("pt", n - 1), 6, "pt_ready", n)
                self.take(("o", n - 1), 7, "o_ready", n)
            for part in PARTS[3 * n:3 * n + 3]:
                for job, k in part:
                    if job[0] == "mix":
                        self.mix(job[1])
                    elif k == 0 and job[0] == "proj":
                        self.proj(job[1], job[2])
                    elif k == 0:
                        self.take(job, 1 - job[1] % 2, "u_ready", 8 - job[1])
        for j in range(2):
            self.mix(j)
        for j in range(4):
            self.take(("mt", j), 4 + j, "mT_ready", j + 1)
        self.gate0 = list(self.fills)
        self.fills = [n + GATE_STEPS * GATE_FILLS for n in self.fills]
        self.reader = [("x_added", 16 * GATE_STEPS + b + 1 - 8) for b in range(8)]
        self.norm(2)
        self.ffn0 = list(self.fills)
        self.total = [n + FFN_STEPS * FFN_FILLS for n in self.fills]

    def norm(self, which):
        for t in range(TT):
            for half in range(2):
                self.take((f"n{which}", t, half), 2 * (t % 4) + half, "htmp_ready",
                          16 * (which - 1) + 2 * t + half + 1)

    def mix(self, j):
        self.take(("mix", j), 2 + j % 2, "mix_read", 2 * (3 - j // 2) + j % 2 + 1)

    def proj(self, g, j):
        bank = j % 2 if j < 8 or g and j >= 14 else 2 + j % 2
        if j < 8:
            self.take(("proj", g, j), bank, "rope_read", 8 * g + j + 1)
        else:
            self.take(("proj", g, j), bank, "v_ready", sum(N_V[:g]) + j - 8 + 1)

    def take(self, name, bank, sem, count):
        self.fills[bank] += 1
        self.job[name] = (bank, self.fills[bank])
        self.before[name] = self.reader[bank]
        self.reader[bank] = (sem, count)


GATE_STEPS, GATE_FILLS = 4, 4
FFN_STEPS, FFN_FILLS = FF_TILES // 2, 3
PLAN = Plan()
CHUNKS = []
for _g in range(GROUPS):
    CHUNKS += [(0, ("q", _g, 0), ("proj", _g, 2 if _g == 0 else 1)), (1, ("q", _g, 1), ("proj", _g, 3)),
               (2, ("v", _g, 0), ("proj", _g, 7 + N_V[_g])), (3, ("v", _g, 1), ("proj", _g, 7 + N_V[_g])),
               (0, ("k", _g, 0), ("proj", _g, 5)), (1, ("k", _g, 1), ("proj", _g, 7))]
CHUNKS += [(0, ("u", 3), ("u", 6)), (1, ("u", 2), ("u", 4)), (2, ("maps", 1), ("mix", 5)),
           (3, ("maps", 0), ("mix", 1)), (0, ("u", 1), ("u", 2)), (1, ("u", 0), ("u", 0))]
F_PROJ, F_GATE, F_FFN = sum(c[0] == 0 for c in CHUNKS), 3, 2
D_PROJ = sum(c[0] == 2 for c in CHUNKS)
F_TOTAL = F_PROJ + F_GATE * GATE_STEPS + F_FFN * FFN_STEPS
D_TOTAL = D_PROJ + GATE_STEPS + FFN_STEPS
RAW_PROJ = len(CHUNKS) // 2
DVE_STEPS = 129
RAW_TOTAL = RAW_PROJ + 5 * GATE_STEPS + 3 * FFN_STEPS


def order(g, j):
    if g == 0 and j < 4:
        return j % 2, j // 2
    return j // 2, j % 2


class Chain:

    def __init__(self, eng, sem):
        self.eng, self.sem, self.base, self.n = eng, sem, 0, 0

    def link(self, ins):
        self.n += 1
        ins.then_inc(self.sem, 1)
        self.eng.wait_ge(self.sem, self.base + self.n)

    def enter(self, i, per):
        saved = (self.base, self.n)
        self.base, self.n = self.base + self.n + i * per, 0
        return saved

    def leave(self, saved, steps, per):
        assert self.n == per, ("steps in the loop", self.n, per)
        self.base, self.n = saved[0], saved[1] + steps * per


def encoder(nc, x, w_in, maps, w_up_pool, w_up_attn, w_gate, w_out, w_fg, w_fu, w_fd,
            norm_mix, norm_ffn, norm_final, pool_scale, b_gate,
            rope, masks, diag, ident, edge, scratch, out):
    ctx = ExitStack()
    with ctx:
        def sem(name):
            return ctx.enter_context(nc.semaphore(name))

        base = 16512

        def at(name, offset, shape, dt=F32):
            return nc.alloc_sbuf_tensor_at(name, [P] + shape, dt, offset=base + offset)

        h_hi, h_lo = at("h_hi", 0, [KD, T], F32R), at("h_lo", 32768, [KD, T], F32R)
        SLOT = 65536
        w_hi = [at(f"w_hi{s}", SLOT + 8192 * s, [D], F32R) for s in range(4)]
        w_lo = [at(f"w_lo{s}", SLOT + 8192 * s + 4096, [D], F32R) for s in range(4)]
        raw = [at(f"raw{r}", SLOT + 32768 + 4096 * r, [D]) for r in range(2)]
        XR = SLOT + 40960
        X = at("X", XR, [TT, D])
        qk = [at("qk_even", XR, [4, T]), at("qk_odd", XR + 16384, [4, T])]
        U = at("U", XR + 16384, [POOL_GROUPS, T + 16])
        YR = XR + 32768
        y_hi = [at(f"y_hi{j}", YR + 8192 * j, [T], F32R) for j in range(2)]
        y_lo = [at(f"y_lo{j}", YR + 8192 * j + 4096, [T], F32R) for j in range(2)]
        rope_sb = at("rope_sb", YR, [2, T])
        rec = [at("rec0", XR, [4, 6, REC]), at("rec1", YR + 512, [4, 6, REC])]
        masks_sb, diag_sb = at("masks_sb", YR + 8192, [3, 256]), at("diag_sb", YR + 11264, [P])
        MR = YR + 16384
        V = [at("V_even", MR, [11, 256]), at("V_odd", MR + 11264, [8, 256])]
        pool_hi, pool_lo = at("pool_hi", MR + 11264, [T], F32R), at("pool_lo", MR + 15360, [T], F32R)
        masked = at("masked", MR + 19456, [2, 256])
        prob = at("prob", MR + 21504, [2, 2, 256])
        probT = at("probT", MR + 25600, [4, P])
        r_sh, r_c, r_s = (at(f"rope_t{i}", MR + 27648 + 2048 * i, [H2]) for i in range(3))
        o_st = at("o_st", MR + 33792, [4, REC])
        pw0, pw1, pooled = (at("pw0", MR + 35904, [1040]), at("pw1", MR + 40064, [1040]),
                            at("pooled", MR + 44224, [T]))
        mix_hi, mix_lo = at("mix_hi", MR, [4, T], F32R), at("mix_lo", MR + 16384, [4, T], F32R)
        m_hi, m_lo = at("m_hi", MR + 32768, [2, T], F32R), at("m_lo", MR + 40960, [2, T], F32R)
        squares, xn = at("squares", MR, [D]), at("xn", MR + 4096, [2, D])
        n_tmp = at("n_tmp", MR + 12288, [2, 4, P])
        g_fin, fin = at("g_fin", MR + 16384, [D]), at("fin", MR + 20480, [2, D])
        SR = MR + 49152
        act_t = at("act_t", SR, [3, H2])
        off = [SR + 6144]

        def small(name, shape):
            n = int(np.prod(shape)) * 4
            o = off[0]
            off[0] = o + (n + 31) // 32 * 32
            return at(name, o, shape)

        ident_sb = small("ident_sb", [P])
        g_mix, g_ffn = small("g_mix", [KD]), small("g_ffn", [KD])
        p_scale, b_g, edge_sb = small("p_scale", [4]), small("b_g", [16]), small("edge_sb", [4, 16])
        zero, eps, b_now = small("zero", [1]), small("eps", [1]), small("b_now", [2])
        ss, std, rstd, mx = small("ss", [2]), small("std", [2]), small("rstd", [2]), small("mx", [2])
        mn, den, rden = (at(name, SR + 64 * i, [16]) for i, name in enumerate(("mn", "den", "rden")))
        d3, e3, wd, coef = (at(name, SR + 192 * (i + 1), [3, 16]) for i, name in enumerate(("d3", "e3", "wd", "coef")))
        assert base + off[0] <= nc.sbuf_usable_end
        ps = ctx.enter_context(nc.psum_tensor("ps", [P, 8, H2], F32))

        bank_full = [sem(f"bank_full{b}") for b in range(8)]
        raw_in = [sem(f"raw_in{r}") for r in range(2)]
        w_ready = [sem(f"w_ready{s}") for s in range(4)]
        w_hi_done, zeroed, eps_set, const_in, dve_chain = (
            sem(n) for n in ("w_hi_done", "zeroed", "eps_set", "const_in", "dve_chain"))
        sems = {name: sem(name) for name in PER_SEQ}
        (ss_ready, std_ready, xn_ready, htmp_ready, hhi_ready, h_ready, rope_read, qk_ready, v_ready, s_read,
         negmax_ready, p_ready, pt_ready, o_ready, u_ready, pooled_ready, pool_hi_ready, pool_ready, mix_read,
         mix_hi_ready, mixed_ready, diff_ready, weight_ready, merged, mhi_ready, mT_ready, a_read, b_read, sig_ready, y_sum, yhi_ready,
         y_ready, x_added, fin_ready, bias_ready, tab_in, gfin_in) = (
            sems[name] for name in PER_SEQ if not name[-1].isdigit())
        x_in = [sems[f"x_in{t}"] for t in range(TT)]
        rec_in = [sems[f"rec_in{t}"] for t in range(2)]
        o_stored = [sems[f"o_stored{t}"] for t in range(4)]
        out_stored = [sems[f"out_stored{t}"] for t in range(2)]

        def filled(s, b, n):
            return s * PLAN.total[b] + (CREDIT["bank_full"] + n)

        def split_by(s, slot, n):
            return s * (F_TOTAL if slot < 2 else D_TOTAL) + (CREDIT["w_ready"] + n)

        x_t = x.rearrange("s (t p) d -> s t p d", p=P)
        out_t = out.rearrange("s (t p) d -> s t p d", p=P)
        block = ctx.enter_context(nc.Block())

        @block.sync
        def _(sp):
            def cols(w):
                return w.rearrange("(k p) c -> p k c", p=P)

            w_in_c, w_gate_c = cols(w_in), cols(w_gate)
            upp_c, upa_c, fg_c, fu_c = cols(w_up_pool), cols(w_up_attn), cols(w_fg), cols(w_fu)
            w_out_r = w_out.rearrange("(k p) c -> k p c", p=P)
            w_fd_r = w_fd.rearrange("(k p) c -> k p c", p=P)
            maps_c = maps.rearrange("g c d -> c g d")

            def r3(r, n):
                return raw[r][:, 0:n * P].rearrange("p (k c) -> p k c", c=P)

            def raws_free(s, i, r):
                cols_split = sp.snap(s * F_TOTAL + (i * F_GATE + (F_PROJ + 1)))
                rows_split = sp.snap(s * D_TOTAL + (i + (D_PROJ + 1)))
                sp.wait_ge(w_ready[r], cols_split)
                sp.wait_ge(w_ready[2 + r], rows_split)

            with sp.Fori(0, SEQS) as s:
                done = [0] * 4
                for c, (slot, what, _) in enumerate(CHUNKS):
                    r, kind = c % 2, what[0]
                    if c < 2:
                        sp.wait_ge(w_ready[2 + c], split_by(s, 2 + c, 0))
                    else:
                        before = CHUNKS[c - 2][0]
                        sp.wait_ge(w_ready[before], split_by(s, before, done[before]))
                    done[slot] += 1
                    if kind == "u":
                        src, dst = w_in_c[:, :, P * what[1]:P * what[1] + P], r3(r, 8)
                    elif kind == "maps":
                        src, dst = maps_c[:, 2 * what[1]:2 * what[1] + 2, :], r3(r, 2)
                    elif kind == "v":
                        at_c = PW + 2 * AW + 256 * what[1]
                        src = w_in_c[:, 4 * what[2]:4 * what[2] + 4, at_c:at_c + 256]
                        dst = raw[r][:, :].rearrange("p (k c) -> p k c", c=256)
                    else:
                        at_c = PW + (AW if kind == "k" else 0) + 256 * what[1] + P * what[2]
                        src, dst = w_in_c[:, :, at_c:at_c + P], r3(r, 8)
                    sp.dma_start(dst, src).then_inc(raw_in[r], 16)
                with sp.Fori(0, GATE_STEPS) as i:
                    for j in range(2):
                        up, ga, gb = (3 * j) % 2, (3 * j + 1) % 2, (3 * j + 2) % 2
                        col = bass.ds(i * 256 + P * j, P)
                        if j == 0:
                            raws_free(s, i, 0)
                        else:
                            sp.wait_ge(w_ready[1], split_by(s, 1, F_PROJ + i * F_GATE + 1))
                        sp.dma_start(r3(up, 4), upp_c[:, :, col]).then_inc(raw_in[up], 16)
                        sp.dma_start(raw[up][:, 4 * P:6 * P].rearrange("p (k c) -> p k c", c=P),
                                     upa_c[:, :, col]).then_inc(raw_in[up], 16)
                        if j == 0:
                            raws_free(s, i, 1)
                        else:
                            sp.wait_ge(w_ready[0], split_by(s, 0, F_PROJ + i * F_GATE + 2))
                        sp.dma_start(r3(ga, 8), w_gate_c[:, :, col]).then_inc(raw_in[ga], 16)
                        sp.wait_ge(w_ready[up], split_by(s, up, F_PROJ + i * F_GATE + (1 if j == 0 else 2)))
                        sp.dma_start(r3(gb, 8), w_gate_c[:, :, bass.ds(i * 256 + P * j + D, P)]
                                     ).then_inc(raw_in[gb], 16)
                    for j in range(2):
                        sp.wait_ge(w_ready[j], split_by(s, j, F_PROJ + i * F_GATE + 3))
                        sp.dma_start(raw[j][:, :], w_out_r[i * 2 + j]).then_inc(raw_in[j], 16)
                f0 = F_PROJ + GATE_STEPS * F_GATE
                with sp.Fori(0, FFN_STEPS) as i:
                    for j in range(2):
                        col = bass.ds(i * 256 + P * j, P)
                        for k, w in enumerate((fg_c, fu_c)):
                            if j == 0:
                                sp.wait_ge(w_ready[2 + k], s * D_TOTAL + i + (1 + D_PROJ + GATE_STEPS))
                            else:
                                sp.wait_ge(w_ready[k], split_by(s, k, f0 + i * F_FFN + 1))
                            sp.dma_start(r3(k, 8), w[:, :, col]).then_inc(raw_in[k], 16)
                    for j in range(2):
                        sp.wait_ge(w_ready[j], split_by(s, j, f0 + i * F_FFN + 2))
                        sp.dma_start(raw[j][:, :], w_fd_r[i * 2 + j]).then_inc(raw_in[j], 16)

        @block.gpsimd
        def _(pool):
            chain = Chain(pool, w_hi_done)
            for s4 in range(4):
                pool.sem_inc(w_ready[s4], 1)
            nc.gpsimd.memset(zero[:, :], 0.0).then_inc(zeroed, 1)
            pool.wait_ge(zeroed, 1)

            def split(s, r, n_raw, slot, width=D):
                pool.wait_ge(raw_in[r], (s * RAW_TOTAL + n_raw) * 16)
                chain.link(nc.gpsimd.tensor_tensor(w_hi[slot][:, 0:width], raw[r][:, 0:width],
                                                   zero[:, :].broadcast_to([P, width]), ALU.add))
                nc.gpsimd.tensor_tensor(w_lo[slot][:, 0:width], raw[r][:, 0:width],
                                        w_hi[slot][:, 0:width].bitcast(F32), ALU.subtract
                                        ).then_inc(w_ready[slot], 1)

            SPLITS = len(CHUNKS) + 8 * GATE_STEPS + 6 * FFN_STEPS
            with pool.Fori(0, SEQS) as s:
                saved = chain.enter(s, SPLITS)
                last_use = {}
                for c, (slot, what, job) in enumerate(CHUNKS):
                    if slot in last_use:
                        b, n = PLAN.job[last_use[slot]]
                        pool.wait_ge(bank_full[b], filled(s, b, n))
                    else:
                        b, n = ((5, -2), (7, -2), (0, 0), (7, 0))[slot]
                        pool.wait_ge(bank_full[b], filled(s, b, n))
                    last_use[slot] = job
                    split(s, c % 2, c // 2 + 1, slot, 2 * P if what[0] == "maps" else D)
                for g in range(POOL_GROUPS):
                    pool.wait_ge(mix_hi_ready, due("mix_hi_ready", s, g + 1))
                    nc.gpsimd.tensor_tensor(mix_lo[:, g, :], U[:, g, 8:8 + T], mix_hi[:, g, :].bitcast(F32),
                                            ALU.subtract).then_inc(mixed_ready, 1)
                with pool.Fori(0, GATE_STEPS) as i:
                    inner = chain.enter(i, 8)

                    def gate_use(b, n):
                        pool.wait_ge(bank_full[b], filled(s, b, PLAN.gate0[b] + i * GATE_FILLS + n))

                    r0 = RAW_PROJ + i * 5
                    b, n = PLAN.job["u", 2]
                    pool.wait_ge(bank_full[b], filled(s, b, n))
                    gate_use(5, -2)
                    split(s, 0, r0 + 2, 0, 6 * P)
                    b, n = PLAN.job["u", 0]
                    pool.wait_ge(bank_full[b], filled(s, b, n))
                    gate_use(7, -2)
                    split(s, 1, r0 + 1, 1)
                    gate_use(3, 1)
                    split(s, 0, r0 + 3, 0)
                    gate_use(5, 1)
                    split(s, 1, r0 + 3, 1, 6 * P)
                    gate_use(7, 1)
                    split(s, 0, r0 + 4, 0)
                    gate_use(3, 2)
                    split(s, 1, r0 + 4, 1)
                    b, n = PLAN.job["mix", 5]
                    pool.wait_ge(bank_full[b], filled(s, b, n))
                    gate_use(0, 0)
                    split(s, 0, r0 + 5, 2)
                    gate_use(7, 0)
                    split(s, 1, r0 + 5, 3)
                    chain.leave(inner, GATE_STEPS, 8)
                with pool.Fori(0, FFN_STEPS) as i:
                    inner = chain.enter(i, 6)

                    def ffn_use(b, n):
                        pool.wait_ge(bank_full[b], filled(s, b, PLAN.ffn0[b] + i * FFN_FILLS + n))

                    r0 = RAW_PROJ + GATE_STEPS * 5 + i * 3
                    ffn_use(5, -2)
                    split(s, 0, r0 + 1, 0)
                    ffn_use(7, -2)
                    split(s, 1, r0 + 1, 1)
                    ffn_use(1, 1)
                    split(s, 0, r0 + 2, 0)
                    ffn_use(3, 1)
                    split(s, 1, r0 + 2, 1)
                    ffn_use(0, 0)
                    split(s, 0, r0 + 3, 2)
                    ffn_use(7, 0)
                    split(s, 1, r0 + 3, 3)
                    chain.leave(inner, FFN_STEPS, 6)
                chain.leave(saved, SEQS, SPLITS)

        @block.tensor
        def _(pe):
            for b in range(8):
                pe.sem_inc(bank_full[b], CREDIT["bank_full"])
            pe.wait_ge(const_in, 16 * 6)

            def col_job(bank, slot, half, ks, first, last, rhs=(h_hi, h_lo), w0=0):
                o = ps[:, bank, :]
                for k in ks:
                    wh = w_hi[slot][:, (w0 + k) * P:(w0 + k + 1) * P]
                    wl = w_lo[slot][:, (w0 + k) * P:(w0 + k + 1) * P]
                    rh, rl = (r[:, k, half * H2:(half + 1) * H2] for r in rhs)
                    nc.tensor.matmul(o, wh, rh, start=(k == first), stop=False)
                    nc.tensor.matmul(o, wh, rl, start=False, stop=False)
                    ins = nc.tensor.matmul(o, wl, rh, start=False, stop=(k == last))
                if ks[-1] == last:
                    ins.then_inc(bank_full[bank], 1)

            def perm(hx, k, g, first):
                d, n = DIL[g], T // DIL[g]
                return hx[:, k, :].rearrange("p (i r) -> p r i", r=d)[:, first // n, first % n:first % n + P]

            def v_job(bank, g, v, ks):
                o = ps[:, bank, 0:256]
                first = v_tokens(g)[v]
                for k in ks:
                    slot, kk = 2 + k // 4, k % 4
                    rh = w_hi[slot][:, kk * 256:(kk + 1) * 256]
                    rl = w_lo[slot][:, kk * 256:(kk + 1) * 256]
                    lh, ll = perm(h_hi, k, g, first), perm(h_lo, k, g, first)
                    nc.tensor.matmul(o, lh, rh, start=(k == 0), stop=False)
                    nc.tensor.matmul(o, lh, rl, start=False, stop=False)
                    ins = nc.tensor.matmul(o, ll, rh, start=False, stop=(k == KD - 1))
                if ks[-1] == KD - 1:
                    ins.then_inc(bank_full[bank], 1)

            def proj_steps(s, job, ks):
                j, bank = job[-1], PLAN.job[job][0]
                if ks[0] == 0:
                    reader, n = PLAN.before[job]
                    pe.wait_ge(sems[reader], due(reader, s, n))
                if job[0] == "u":
                    tile, half, chunks = 3 - j // 2, j % 2, 2 * GROUPS
                    begins = half == 1
                elif j < 8:
                    (tile, half), chunks = order(job[1], j), 2 * job[1]
                    begins = half == 0
                else:
                    if ks[0] == 0:
                        pe.wait_ge(w_ready[2], split_by(s, 2, job[1] + 1))
                        pe.wait_ge(w_ready[3], split_by(s, 3, job[1] + 1))
                    v_job(bank, job[1], j - 8, ks)
                    return
                if ks[0] == 0 and begins:
                    pe.wait_ge(w_ready[tile % 2], split_by(s, tile % 2, chunks + tile // 2 + 1))
                if job in (("proj", 0, 0), ("proj", 0, 2)) and ks[0] == 0:
                    pe.wait_ge(h_ready, due("h_ready", s, 8 * (half + 1)))
                col_job(bank, tile % 2, half, ks, 0, KD - 1)

            def projections(s, part):
                for job, k in PARTS[part]:
                    if job[0] == "mix":
                        mix_job(s, job[1])
                    else:
                        proj_steps(s, job, [k])

            def mix_job(s, j):
                g, half = j // 2, j % 2
                b = PLAN.job["mix", j][0]
                reader, n = PLAN.before["mix", j]
                pe.wait_ge(sems[reader], due(reader, s, n))
                slot = 3 - g // 2
                if half == 0:
                    pe.wait_ge(pool_ready, due("pool_ready", s, POOL_GROUPS - g))
                    if g % 2:
                        pe.wait_ge(w_ready[slot], split_by(s, slot, D_PROJ))
                o, m = ps[:, b, :], slice((g % 2) * P, (g % 2 + 1) * P)
                tok = slice(half * H2, (half + 1) * H2)
                nc.tensor.matmul(o, w_hi[slot][:, m], pool_hi[:, tok], start=True, stop=False)
                nc.tensor.matmul(o, w_hi[slot][:, m], pool_lo[:, tok], start=False, stop=False)
                nc.tensor.matmul(o, w_lo[slot][:, m], pool_hi[:, tok], start=False, stop=True
                                 ).then_inc(bank_full[b], 1)

            def norm_transposes(s, which, tiles):
                for t in tiles:
                    pe.wait_ge(xn_ready, due("xn_ready", s, 8 * (which - 1) + t + 1))
                    for half in range(2):
                        b = PLAN.job[f"n{which}", t, half][0]
                        reader, n = PLAN.before[f"n{which}", t, half]
                        pe.wait_ge(sems[reader], due(reader, s, n))
                        for k in range(4):
                            c = (4 * half + k) * P
                            ins = nc.tensor.transpose(ps[:, b, k * P:(k + 1) * P], xn[:, t % 2, c:c + P],
                                                      ident_sb[:, :])
                        ins.then_inc(bank_full[b], 1)

            def scores(s, unit):
                g, u = unit // UNITS, unit % UNITS
                pair, b = u // TT, u % TT
                lo, wid, _, _ = window(g, b)
                if u == 0:
                    pe.wait_ge(qk_ready, due("qk_ready", s, 8 * (g + 1)))
                for h in range(2):
                    bank = PLAN.job["s", unit, h][0]
                    reader, n = PLAN.before["s", unit, h]
                    pe.wait_ge(sems[reader], due(reader, s, n))
                    rows = slice(HEAD * h, HEAD * h + HEAD)
                    nc.tensor.matmul(ps[:, bank, 0:wid], qk[g % 2][rows, pair, b * P:(b + 1) * P],
                                     qk[g % 2][rows, 2 + pair, lo:lo + wid], start=True, stop=True
                                     ).then_inc(bank_full[bank], 1)

            def prob_transposes(s, unit):
                g, u = unit // UNITS, unit % UNITS
                wid = window(g, u % TT)[1]
                pe.wait_ge(p_ready, due("p_ready", s, unit + 1))
                bank = PLAN.job["pt", unit][0]
                reader, n = PLAN.before["pt", unit]
                pe.wait_ge(sems[reader], due(reader, s, n))
                n = 0
                for h in range(2):
                    for c in range(wid // P):
                        ins = nc.tensor.transpose(ps[:, bank, n * P:(n + 1) * P],
                                                  prob[:, u % 2, h, c * P:(c + 1) * P], ident_sb[:, :])
                        n += 1
                ins.then_inc(bank_full[bank], 1)

            def prob_v(s, unit):
                g, u = unit // UNITS, unit % UNITS
                pair = u // TT
                tiles = window(g, u % TT)[2]
                if u == 0:
                    pe.wait_ge(v_ready, due("v_ready", s, sum(N_V[:g + 1])))
                pe.wait_ge(pt_ready, due("pt_ready", s, unit + 1))
                bank = PLAN.job["o", unit][0]
                reader, n = PLAN.before["o", unit]
                pe.wait_ge(sems[reader], due(reader, s, n))
                n = 0
                for h in range(2):
                    e = (2 * pair + h) * HEAD
                    for c, v in enumerate(tiles):
                        ins = nc.tensor.matmul(ps[:, bank, h * HEAD:(h + 1) * HEAD], probT[:, n, :],
                                               V[g % 2][:, v, e:e + HEAD], start=(c == 0),
                                               stop=(c == len(tiles) - 1))
                        n += 1
                ins.then_inc(bank_full[bank], 1)

            def row_step(s, n_w, n_y, n_x, reader):
                for rnd in range(2):
                    for j in range(2):
                        if rnd == 0:
                            pe.wait_ge(w_ready[2 + j], split_by(s, 2 + j, n_w))
                            pe.wait_ge(y_ready, due("y_ready", s, n_y + 2 * j + 2))
                        for b in range(8):
                            t, n = (8 * rnd + b) // 2, b % 2
                            if j == 0 and rnd == 0:
                                pe.wait_ge(sems[reader[b][0]], due(reader[b][0], s, reader[b][1]))
                            elif j == 0:
                                pe.wait_ge(x_added, due("x_added", s, n_x + b + 1))
                            o = ps[:, b, :]
                            tok, col = slice(t * P, (t + 1) * P), slice(n * H2, (n + 1) * H2)
                            nc.tensor.matmul(o, y_hi[j][:, tok], w_hi[2 + j][:, col], start=(j == 0), stop=False)
                            nc.tensor.matmul(o, y_hi[j][:, tok], w_lo[2 + j][:, col], start=False, stop=False)
                            ins = nc.tensor.matmul(o, y_lo[j][:, tok], w_hi[2 + j][:, col],
                                                   start=False, stop=(j == 1))
                            if j == 1:
                                ins.then_inc(bank_full[b], 1)

            with pe.Fori(0, SEQS) as s:
                norm_transposes(s, 1, range(5))
                for n, t in enumerate((5, 6, 7)):
                    proj_steps(s, ("proj", 0, n // 2), range(4 * (n % 2), 4 * (n % 2) + 4))
                    norm_transposes(s, 1, [t])
                proj_steps(s, ("proj", 0, 1), range(4, 8))
                for j in range(2, 8 + N_V[0]):
                    proj_steps(s, ("proj", 0, j), range(KD))
                for unit in range(GROUPS * UNITS + 1):
                    busy = unit < GROUPS * UNITS
                    if busy:
                        scores(s, unit)
                    projections(s, 3 * unit)
                    if unit:
                        prob_transposes(s, unit - 1)
                    projections(s, 3 * unit + 1)
                    if unit:
                        prob_v(s, unit - 1)
                    projections(s, 3 * unit + 2)
                for half in range(2):
                    mix_job(s, half)
                for batch in range(2):
                    pe.wait_ge(merged, due("merged", s, batch + 1))
                    for pair in range(2):
                        job = ("mt", 2 * batch + pair)
                        b = PLAN.job[job][0]
                        reader, n = PLAN.before[job]
                        pe.wait_ge(sems[reader], due(reader, s, n))
                        for t in range(4):
                            ins = nc.tensor.transpose(ps[:, b, t * P:(t + 1) * P],
                                                      rec[batch][:, t, pair, 0:2 * HEAD], ident_sb[:, :])
                        ins.then_inc(bank_full[b], 1)
                with pe.Fori(0, GATE_STEPS) as i:
                    pe.wait_ge(mixed_ready, due("mixed_ready", s, POOL_GROUPS))
                    pe.wait_ge(mT_ready, due("mT_ready", s, 4))
                    for j in range(2):
                        slots = [(3 * j + c) % 2 for c in range(3)]
                        counts = [(1, 1, 2), (2, 3, 3)][j]
                        f = i * 2 + (j - 1)

                        def bank_read(b, name, n):
                            if j == 0:
                                pe.wait_ge(x_added, due("x_added", s, i * 16 + (b + 1 - 8)))
                            else:
                                pe.wait_ge(sems[name], due(name, s, n))

                        for c in range(3):
                            pe.wait_ge(w_ready[slots[c]], split_by(s, slots[c], i * F_GATE + (F_PROJ + counts[c])))
                            for half in range(2):
                                if c == 0:
                                    bank_read(half, "a_read", f * 2 + (half + 1))
                                    col_job(half, slots[0], half, range(4), 0, 3, (mix_hi, mix_lo))
                                else:
                                    b = 2 + 2 * c + half
                                    bank_read(b, "sig_ready", f * 4 + (2 * (c - 1) + half + 1))
                                    col_job(b, slots[c], half, range(KD), 0, KD - 1)
                            for half in range(2):
                                if c == 0:
                                    bank_read(2 + half, "b_read", f * 2 + (half + 1))
                                    col_job(2 + half, slots[0], half, range(2), 0, 1, (m_hi, m_lo), 4)
                    last = i * 2 + 1
                    reader = ([(name, last * 2 + (half + 1)) for name in ("a_read", "b_read") for half in range(2)]
                              + [("sig_ready", last * 4 + (n + 1)) for n in range(4)])
                    row_step(s, i + (D_PROJ + 1), i * 4, i * 16, reader)
                norm_transposes(s, 2, range(TT))
                with pe.Fori(0, FFN_STEPS) as i:
                    pe.wait_ge(htmp_ready, due("htmp_ready", s, 32))
                    for j in range(2):
                        for c in range(2):
                            pe.wait_ge(w_ready[c], split_by(s, c, i * F_FFN + (F_PROJ + GATE_STEPS * F_GATE + j + 1)))
                            for half in range(2):
                                b = 4 * j + 2 * c + half
                                pe.wait_ge(x_added, due("x_added", s, i * 16 + (16 * GATE_STEPS + b + 1 - 8)))
                                if j == 0 and c == 0:
                                    pe.wait_ge(h_ready, due("h_ready", s, 16 + 8 * (half + 1)))
                                col_job(b, c, half, range(KD), 0, KD - 1)
                    reader = [("sig_ready" if (b // 2) % 2 == 0 else "y_sum",
                               (32 if (b // 2) % 2 == 0 else 16) + 2 * (b // 4) + b % 2 + 1 + i * 4) for b in range(8)]
                    row_step(s, i + (D_PROJ + GATE_STEPS + 1), i * 4 + 16, i * 16 + 16 * GATE_STEPS, reader)

        @block.scalar
        def _(act):
            act.sem_inc(p_ready, CREDIT["p_ready"])
            for n in range(2):
                act.sem_inc(out_stored[n], CREDIT[f"out_stored{n}"])
            for dst, src in ((ident_sb[:, :], ident), (g_mix[:, :], norm_mix), (g_ffn[:, :], norm_ffn),
                             (p_scale[:, :], pool_scale), (b_g[:, :], b_gate),
                             (edge_sb[:, :, :], edge)):
                act.dma_start(dst, src).then_inc(const_in, 16)
            act.wait_ge(eps_set, 1)
            act.wait_ge(const_in, 16 * 6)

            def stats(s, n, t):
                nc.scalar.activation(squares[:, :], X[:, t, :], ACT.Square, accum_out=ss[:, t % 2:t % 2 + 1]
                                     ).then_inc(ss_ready, 1)
                act.wait_ge(ss_ready, due("ss_ready", s, n))
                nc.scalar.activation(std[:, t % 2:t % 2 + 1], ss[:, t % 2:t % 2 + 1], ACT.Sqrt,
                                     bias=eps[:, :], scale=1.0 / D).then_inc(std_ready, 1)

            def round_h(s, which, t):
                for half in range(2):
                    act.wait_ge(htmp_ready, due("htmp_ready", s, 16 * (which - 1) + 2 * t + half + 1))
                    nc.scalar.copy(h_hi[:, 4 * half:4 * half + 4, t * P:(t + 1) * P], n_tmp[:, half, :, :]
                                   ).then_inc(hhi_ready, 1)

            def evict_v(s, g, v):
                b, n = PLAN.job["proj", g, 8 + v]
                act.wait_ge(bank_full[b], filled(s, b, n))
                nc.scalar.copy(V[g % 2][:, v, :], ps[:, b, 0:256]).then_inc(v_ready, 1)

            def exp_unit(s, unit):
                u = unit
                wid = window(unit // UNITS, unit % TT)[1]
                act.wait_ge(negmax_ready, due("negmax_ready", s, unit + 1))
                for h in range(2):
                    ins = nc.scalar.activation(prob[:, u % 2, h, 0:wid], masked[:, h, 0:wid], ACT.Exp,
                                               bias=o_st[:, u % 4, 2 * HEAD + h:2 * HEAD + h + 1],
                                               scale=HEAD ** -0.5,
                                               accum_out=o_st[:, u % 4, 2 * HEAD + 2 + h:2 * HEAD + 3 + h])
                ins.then_inc(p_ready, 1)

            def evict_probs(s, unit):
                wid = window(unit // UNITS, unit % TT)[1]
                b, n = PLAN.job["pt", unit]
                act.wait_ge(bank_full[b], filled(s, b, n))
                nc.scalar.copy(probT[:, 0:2 * wid // P, :],
                               ps[:, b, 0:2 * wid].rearrange("p (n q) -> p n q", q=P)
                               ).then_inc(pt_ready, 1)

            def evict_unit(s, unit):
                g, u = unit // UNITS, unit % UNITS
                b, n = PLAN.job["o", unit]
                act.wait_ge(bank_full[b], filled(s, b, n))
                nc.scalar.copy(o_st[:, u % 4, 0:2 * HEAD], ps[:, b, 0:2 * HEAD]).then_inc(o_ready, 1)
                act.wait_ge(o_ready, due("o_ready", s, unit + 1))
                pair, qb = u // TT, u % TT
                by_res = scratch[2 * g + pair].rearrange("(i r) c -> r i c", r=DIL[g])
                n = T // DIL[g] // P
                act.dma_start(by_res[qb // n, (qb % n) * P:(qb % n + 1) * P, :], o_st[:, u % 4, :]
                              ).then_inc(o_stored[u % 4], 16)

            def load_rec(s, t):
                act.dma_start(rec[t // 4][:, t % 4, :, :], scratch[:, t * P:(t + 1) * P, :].rearrange("q t c -> t q c")
                              ).then_inc(rec_in[t // 4], 16)

            def evict_mix(s, j):
                g, half = j // 2, j % 2
                b, n = PLAN.job["mix", j]
                act.wait_ge(bank_full[b], filled(s, b, n))
                nc.scalar.activation(U[:, g, 8 + half * H2:8 + (half + 1) * H2], ps[:, b, :], ACT.Identity,
                                     scale=p_scale[:, g:g + 1]).then_inc(mix_read, 1)

            def round_pooled(s, g):
                act.wait_ge(pooled_ready, due("pooled_ready", s, POOL_GROUPS - g))
                nc.scalar.copy(pool_hi[:, :], pooled[:, :]).then_inc(pool_hi_ready, 1)

            with act.Fori(0, SEQS) as s:
                for t in range(TT):
                    act.dma_start(X[:, t, :], x_t[s, t]).then_inc(x_in[t], 16)
                for dst, src in ((rope_sb[:, :, :], rope), (masks_sb[:, :, :], masks), (diag_sb[:, :], diag)):
                    act.dma_start(dst, src).then_inc(tab_in, 16)
                for t in range(TT + 1):
                    if t < TT:
                        act.wait_ge(x_in[t], due(f"x_in{t}", s, 1))
                        stats(s, t + 1, t)
                    if t:
                        round_h(s, 1, t - 1)
                for n in range(2):
                    act.wait_ge(out_stored[n], due(f"out_stored{n}", s, 0))
                for v in range(N_V[0]):
                    evict_v(s, 0, v)
                for unit in range(GROUPS * UNITS + 1):
                    if unit:
                        evict_probs(s, unit - 1)
                    if unit < GROUPS * UNITS:
                        exp_unit(s, unit)
                    if unit:
                        evict_unit(s, unit - 1)
                        for job in done(3 * unit - 1, 3 * unit + 1):
                            if job[0] == "u":
                                b, n = PLAN.job[job]
                                j = job[1]
                                act.wait_ge(bank_full[b], filled(s, b, n))
                                nc.scalar.copy(U[:, j // 2, 8 + (j % 2) * H2:8 + (j % 2 + 1) * H2], ps[:, b, :]
                                               ).then_inc(u_ready, 1)
                            elif job[0] == "mix":
                                evict_mix(s, job[1])
                            elif job[2] >= 8:
                                evict_v(s, job[1], job[2] - 8)
                    if unit in POOL_ACT:
                        round_pooled(s, POOL_ACT[unit])
                round_pooled(s, 0)
                for n in range(4):
                    act.wait_ge(o_stored[n], due(f"o_stored{n}", s, 12))
                for t in range(TT):
                    load_rec(s, t)
                for half in range(2):
                    evict_mix(s, half)
                for g in range(POOL_GROUPS):
                    act.wait_ge(mix_read, due("mix_read", s, 8))
                    nc.scalar.copy(mix_hi[:, g, :], U[:, g, 8:8 + T]).then_inc(mix_hi_ready, 1)
                for batch in range(2):
                    act.wait_ge(diff_ready, due("diff_ready", s, batch + 1))
                    nc.scalar.activation(e3[:, :, :], d3[:, :, :], ACT.Exp).then_inc(weight_ready, 1)
                for j in range(4):
                    b, n = PLAN.job["mt", j]
                    act.wait_ge(bank_full[b], filled(s, b, n))
                    nc.scalar.copy(m_hi[:, j % 2, (j // 2) * H2:(j // 2 + 1) * H2], ps[:, b, :]
                                   ).then_inc(mhi_ready, 1)
                act.wait_ge(mixed_ready, due("mixed_ready", s, POOL_GROUPS))
                for t in range(TT):
                    act.dma_start(X[:, t, :], x_t[s, t]).then_inc(x_in[t], 16)
                with act.Fori(0, GATE_STEPS) as i:
                    for j in range(2):
                        f = i * 2 + j
                        nc.scalar.copy(b_now[:, :], b_g[:, :].rearrange("p (g f) -> p f g", g=2)[:, bass.ds(f, 1), :]
                                       .rearrange("p a g -> p (a g)")).then_inc(bias_ready, 1)
                        act.wait_ge(bias_ready, due("bias_ready", s, f + 1))
                        for half in range(2):
                            act.wait_ge(bank_full[4 + half], filled(s, 4 + half, i * GATE_FILLS + (PLAN.gate0[4 + half] + j + 1)))
                            act.wait_ge(y_ready, due("y_ready", s, f * 2 + (half - 1)))
                            nc.scalar.activation(act_t[:, half, :], ps[:, 4 + half, :], ACT.Sigmoid,
                                                 bias=b_now[:, 0:1]).then_inc(sig_ready, 1)
                        for half in range(2):
                            act.wait_ge(bank_full[6 + half], filled(s, 6 + half, i * GATE_FILLS + (PLAN.gate0[6 + half] + j + 1)))
                            act.wait_ge(y_sum, due("y_sum", s, f * 2 + half))
                            nc.scalar.activation(act_t[:, 2, :], ps[:, 6 + half, :], ACT.Sigmoid,
                                                 bias=b_now[:, 1:2]).then_inc(sig_ready, 1)
                            act.wait_ge(y_sum, due("y_sum", s, f * 2 + (half + 1)))
                            nc.scalar.copy(y_hi[j][:, half * H2:(half + 1) * H2], act_t[:, half, :]
                                           ).then_inc(yhi_ready, 1)
                for t in range(TT + 1):
                    if t < TT:
                        act.wait_ge(x_added, due("x_added", s, 16 * GATE_STEPS - 16 + 2 * (t + 1)))
                        if t == 0:
                            act.dma_start(g_fin[:, :], norm_final.partition_broadcast(P)
                                          ).then_inc(gfin_in, 16)
                        stats(s, TT + t + 1, t)
                    if t:
                        round_h(s, 2, t - 1)
                with act.Fori(0, FFN_STEPS) as i:
                    for j in range(2):
                        n = i * 4 + (16 + 2 * j)
                        for half in range(2):
                            act.wait_ge(bank_full[4 * j + half], filled(s, 4 * j + half, i * FFN_FILLS + (PLAN.ffn0[4 * j + half] + 1)))
                            act.wait_ge(y_ready, due("y_ready", s, n + (half - 1)))
                            nc.scalar.activation(act_t[:, half, :], ps[:, 4 * j + half, :], ACT.Silu
                                                 ).then_inc(sig_ready, 1)
                        for half in range(2):
                            act.wait_ge(y_sum, due("y_sum", s, n + (half + 1)))
                            nc.scalar.copy(y_hi[j][:, half * H2:(half + 1) * H2], act_t[:, half, :]
                                           ).then_inc(yhi_ready, 1)
                for t in range(TT + 1):
                    if t < TT:
                        act.wait_ge(x_added, due("x_added", s, PER_SEQ["x_added"] - 16 + 2 * (t + 1)))
                        stats(s, 2 * TT + t + 1, t)
                    if t:
                        act.wait_ge(fin_ready, due("fin_ready", s, t))
                        act.dma_start(out_t[s, t - 1], fin[:, (t - 1) % 2, :]).then_inc(out_stored[(t - 1) % 2], 16)
            for n in range(2):
                act.wait_ge(out_stored[n], due(f"out_stored{n}", SEQS, 0))

        @block.vector
        def _(dve):
            dve.sem_inc(y_sum, CREDIT["y_sum"])
            dve.sem_inc(y_ready, CREDIT["y_ready"])
            dve.sem_inc(x_added, CREDIT["x_added"])
            nc.vector.memset(eps[:, :], EPS).then_inc(eps_set, 1)
            dve.wait_ge(const_in, 16 * 6)
            chain = Chain(dve, dve_chain)
            V_ = nc.vector

            def rsqrt(s, n, t):
                dve.wait_ge(std_ready, due("std_ready", s, n))
                chain.link(V_.reciprocal(rstd[:, t % 2:t % 2 + 1], std[:, t % 2:t % 2 + 1]))

            def norm(s, which, gain):
                for t in range(TT + 1):
                    if t < TT:
                        rsqrt(s, 8 * (which - 1) + t + 1, t)
                        V_.tensor_scalar(xn[:, t % 2, :], X[:, t, :], rstd[:, t % 2:t % 2 + 1], None, ALU.mult
                                         ).then_inc(xn_ready, 1)
                    if t:
                        v = t - 1
                        for half in range(2):
                            if v:
                                dve.wait_ge(h_ready, due("h_ready", s, 16 * (which - 1) + 2 * v + half - 1))
                            b, n = PLAN.job[f"n{which}", v, half]
                            dve.wait_ge(bank_full[b], filled(s, b, n))
                            V_.tensor_tensor(n_tmp[:, half, :, :], ps[:, b, :].rearrange("p (k q) -> p k q", q=P),
                                             gain[:, 4 * half:4 * half + 4].unsqueeze(2).broadcast_to([P, 4, P]),
                                             ALU.mult).then_inc(htmp_ready, 1)
                        for half in range(2):
                            dve.wait_ge(hhi_ready, due("hhi_ready", s, 16 * (which - 1) + 2 * v + half + 1))
                            at_h = (slice(None), slice(4 * half, 4 * half + 4), slice(v * P, (v + 1) * P))
                            V_.tensor_tensor(h_lo[at_h], n_tmp[:, half, :, :], h_hi[at_h].bitcast(F32),
                                             ALU.subtract).then_inc(h_ready, 1)

            partner = [i + 8 if i < 8 else i - 8 if i < 16 else i for i in range(32)]

            def rope_job(s, g, j):
                tile, half = order(g, j)
                if j:
                    dve.wait_ge(qk_ready, due("qk_ready", s, 8 * g + j))
                b, n = PLAN.job["proj", g, j]
                dve.wait_ge(bank_full[b], filled(s, b, n))
                tok = slice(half * H2, (half + 1) * H2)
                V_.tensor_tensor(r_c[:, :], ps[:, b, :], rope_sb[:, 0, tok], ALU.mult)
                chain.link(V_.stream_shuffle(r_sh[:, :], ps[:, b, :], partner))
                V_.tensor_tensor(r_s[:, :], r_sh[:, :], rope_sb[:, 1, tok], ALU.mult).then_inc(rope_read, 1)
                dve.wait_ge(rope_read, due("rope_read", s, 8 * g + j + 1))
                d = DIL[g]
                n = H2 // d
                V_.tensor_tensor(qk[g % 2][:, tile, :].rearrange("p (r i) -> p r i", r=d)[:, :, half * n:(half + 1) * n],
                                 r_c[:, :].rearrange("p (i r) -> p r i", r=d),
                                 r_s[:, :].rearrange("p (i r) -> p r i", r=d), ALU.add
                                 ).then_inc(qk_ready, 1)

            def softmax_unit(s, unit):
                _, wid, _, m = window(unit // UNITS, unit % TT)
                for h in range(2):
                    b, n = PLAN.job["s", unit, h]
                    dve.wait_ge(bank_full[b], filled(s, b, n))
                n = unit
                dve.wait_ge(p_ready, due("p_ready", s, n))
                mask = diag_sb[:, 0:wid] if m == 3 else masks_sb[:, m, 0:wid]
                V_.tensor_tensor(masked[:, :, 0:wid], ps[:, 4:6, 0:wid],
                                 mask.unsqueeze(1).broadcast_to([P, 2, wid]), ALU.add
                                 ).then_inc(s_read, 1)
                dve.wait_ge(s_read, due("s_read", s, n + 1))
                chain.link(V_.reduce_max(mx[:, :], masked[:, :, 0:wid], AX_X))
                if n >= 4:
                    dve.wait_ge(o_stored[n % 4], due(f"o_stored{n % 4}", s, n // 4))
                V_.tensor_scalar(o_st[:, n % 4, 2 * HEAD:2 * HEAD + 2], mx[:, :], -HEAD ** -0.5, None, ALU.mult
                                 ).then_inc(negmax_ready, 1)

            def pool_stage(s, what, g, first=0, last=0):
                n_before = POOL_GROUPS - g
                w, a = 2 << g, 8 - (1 << g)
                sums = [U[:, g, :], pw1, pw0, pw1, pw0]
                if what == "add":
                    if first == 0:
                        dve.wait_ge(u_ready, due("u_ready", s, 2 * n_before))
                    for k in range(first, last + 1):
                        n = T + 16 - (2 << k) + 1
                        chain.link(V_.tensor_tensor(sums[k + 1][:, 0:n], sums[k][:, 0:n],
                                                    sums[k][:, (1 << k):n + (1 << k)], ALU.add))
                elif what == "mean":
                    cur = sums[g + 1]
                    V_.tensor_tensor(cur[:, a:a + 8], cur[:, a:a + 8], edge_sb[:, g, 0:8], ALU.mult)
                    chain.link(V_.tensor_tensor(cur[:, a + 1016:a + 1024], cur[:, a + 1016:a + 1024],
                                                edge_sb[:, g, 8:16], ALU.mult))
                    V_.scalar_tensor_tensor(out=pooled[:, :], in0=cur[:, a:a + T], scalar=1.0 / w,
                                            in1=U[:, g, 8:8 + T], op0=ALU.mult, op1=ALU.subtract
                                            ).then_inc(pooled_ready, 1)
                else:
                    dve.wait_ge(pool_hi_ready, due("pool_hi_ready", s, n_before))
                    V_.tensor_tensor(pool_lo[:, :], pooled[:, :], pool_hi[:, :].bitcast(F32), ALU.subtract
                                     ).then_inc(pool_ready, 1)

            def merge(s, batch):
                dve.wait_ge(rec_in[batch], due(f"rec_in{batch}", s, 4))
                r = rec[batch]

                def heads(a):
                    return a.rearrange("p (t q h) -> p t q h", q=2, h=2)

                neg = [r[:, :, 2 * g:2 * g + 2, 2 * HEAD:2 * HEAD + 2] for g in range(GROUPS)]
                dens = [r[:, :, 2 * g:2 * g + 2, 2 * HEAD + 2:2 * HEAD + 4] for g in range(GROUPS)]
                chain.link(V_.tensor_tensor(heads(mn[:, :]), neg[0], neg[1], ALU.min))
                chain.link(V_.tensor_tensor(heads(mn[:, :]), heads(mn[:, :]), neg[2], ALU.min))
                for g in range(GROUPS):
                    ins = V_.tensor_tensor(heads(d3[:, g, :]), heads(mn[:, :]), neg[g], ALU.subtract)
                ins.then_inc(diff_ready, 1)
                dve.wait_ge(weight_ready, due("weight_ready", s, batch + 1))
                for g in range(GROUPS):
                    ins = V_.tensor_tensor(heads(wd[:, g, :]), heads(e3[:, g, :]), dens[g], ALU.mult)
                chain.link(ins)
                chain.link(V_.tensor_tensor(den[:, :], wd[:, 0, :], wd[:, 1, :], ALU.add))
                chain.link(V_.tensor_tensor(den[:, :], den[:, :], wd[:, 2, :], ALU.add))
                chain.link(V_.reciprocal(rden[:, :], den[:, :]))
                chain.link(V_.tensor_tensor(coef[:, :, :], e3[:, :, :],
                                            rden[:, :].unsqueeze(1).broadcast_to([P, 3, 16]), ALU.mult))
                for g in range(GROUPS):
                    for q in range(2):
                        o = r[:, :, 2 * g + q, 0:2 * HEAD].rearrange("p t (h e) -> p t h e", h=2)
                        c = heads(coef[:, g, :])[:, :, q, :].unsqueeze(3).broadcast_to([P, 4, 2, HEAD])
                        ins = V_.tensor_tensor(o, o, c, ALU.mult)
                chain.link(ins)
                total = r[:, :, 0:2, 0:2 * HEAD]
                chain.link(V_.tensor_tensor(total, total, r[:, :, 2:4, 0:2 * HEAD], ALU.add))
                V_.tensor_tensor(total, total, r[:, :, 4:6, 0:2 * HEAD], ALU.add).then_inc(merged, 1)

            def add_rows(s, i, fills0, fills_step, first):
                for idx in range(16):
                    b, t, n = idx % 8, idx // 2, idx % 2
                    dve.wait_ge(bank_full[b], filled(s, b, i * fills_step + (fills0[b] + first + idx // 8 + 1)))
                    xs = X[:, t, n * H2:(n + 1) * H2]
                    V_.tensor_tensor(xs, xs, ps[:, b, :], ALU.add).then_inc(x_added, 1)

            def y_low(s, j, half, n):
                dve.wait_ge(yhi_ready, due("yhi_ready", s, n))
                tok = slice(half * H2, (half + 1) * H2)
                V_.tensor_tensor(y_lo[j][:, tok], act_t[:, half, :], y_hi[j][:, tok].bitcast(F32), ALU.subtract
                                 ).then_inc(y_ready, 1)

            with dve.Fori(0, SEQS) as s:
                saved = chain.enter(s, DVE_STEPS)
                norm(s, 1, g_mix)
                dve.wait_ge(tab_in, due("tab_in", s, 3))
                for j in range(8):
                    rope_job(s, 0, j)
                for unit in range(GROUPS * UNITS):
                    softmax_unit(s, unit)
                    for job in done(3 * unit - 3, 3 * unit - 1):
                        if job[0] == "proj" and job[2] < 8:
                            rope_job(s, job[1], job[2])
                    if unit == LAST:
                        V_.memset(U[:, :, 0:8], 0.0)
                        chain.link(V_.memset(U[:, :, 8 + T:16 + T], 0.0))
                    for stage in POOL_DVE.get(unit, ()):
                        pool_stage(s, *stage)
                pool_stage(s, "mean", 0)
                pool_stage(s, "lo", 0)

                def merged_low(j):
                    dve.wait_ge(mhi_ready, due("mhi_ready", s, j + 1))
                    tok = slice((j // 2) * H2, (j // 2 + 1) * H2)
                    V_.tensor_tensor(m_lo[:, j % 2, tok], ps[:, 4 + j, :], m_hi[:, j % 2, tok].bitcast(F32),
                                     ALU.subtract).then_inc(mT_ready, 1)

                merge(s, 0)
                merge(s, 1)
                for j in range(4):
                    merged_low(j)
                with dve.Fori(0, GATE_STEPS) as i:
                    for j in range(2):
                        f = i * 2 + j
                        for half in range(2):
                            dve.wait_ge(sig_ready, due("sig_ready", s, f * 4 + (half + 1)))
                            a = act_t[:, half, :]
                            V_.tensor_tensor(a, a, ps[:, half, :], ALU.mult).then_inc(a_read, 1)
                        for half in range(2):
                            dve.wait_ge(sig_ready, due("sig_ready", s, f * 4 + (half + 3)))
                            c = act_t[:, 2, :]
                            V_.tensor_tensor(c, c, ps[:, 2 + half, :], ALU.mult).then_inc(b_read, 1)
                            dve.wait_ge(b_read, due("b_read", s, f * 2 + (half + 1)))
                            a = act_t[:, half, :]
                            V_.tensor_tensor(a, a, c, ALU.add).then_inc(y_sum, 1)
                            y_low(s, j, half, f * 2 + (half + 1))
                    for t in range(TT):
                        dve.wait_ge(x_in[t], due(f"x_in{t}", s, 2))
                    add_rows(s, i, PLAN.gate0, GATE_FILLS, 2)
                norm(s, 2, g_ffn)
                with dve.Fori(0, FFN_STEPS) as i:
                    for j in range(2):
                        for half in range(2):
                            b = 4 * j + 2 + half
                            dve.wait_ge(sig_ready, due("sig_ready", s, i * 4 + (32 + 2 * j + half + 1)))
                            dve.wait_ge(bank_full[b], filled(s, b, i * FFN_FILLS + (PLAN.ffn0[b] + 1)))
                            a = act_t[:, half, :]
                            V_.tensor_tensor(a, a, ps[:, b, :], ALU.mult).then_inc(y_sum, 1)
                        for half in range(2):
                            y_low(s, j, half, i * 4 + (16 + 2 * j + half + 1))
                    add_rows(s, i, PLAN.ffn0, FFN_FILLS, 1)
                dve.wait_ge(gfin_in, due("gfin_in", s, 1))
                for t in range(TT):
                    if t >= 2:
                        dve.wait_ge(out_stored[t % 2], due(f"out_stored{t % 2}", s, t // 2))
                    rsqrt(s, 16 + t + 1, t)
                    V_.scalar_tensor_tensor(out=fin[:, t % 2, :], in0=X[:, t, :], scalar=rstd[:, t % 2:t % 2 + 1],
                                            in1=g_fin[:, :], op0=ALU.mult, op1=ALU.mult
                                            ).then_inc(fin_ready, 1)
                chain.leave(saved, SEQS, DVE_STEPS)


def constants():
    inv = (THETA ** (-np.arange(ROPE_HALF, dtype=np.float32) / ROPE_HALF)).astype(np.float32)
    ang = np.arange(T, dtype=np.float32)[:, None] * inv[None, :]
    cos, sin = np.cos(ang.astype(np.float64)).T, np.sin(ang.astype(np.float64)).T
    rope = np.zeros((P, 2, T), np.float32)
    rope[:, 0] = 1.0
    for h in range(2):
        a, b = HEAD * h, HEAD * h + ROPE_HALF
        rope[a:b, 0], rope[b:b + ROPE_HALF, 0] = cos, cos
        rope[a:b, 1], rope[b:b + ROPE_HALF, 1] = -sin, sin
    q, k = np.arange(P)[:, None], np.arange(256)[None, :]
    masks = np.stack([np.where(np.abs(k - o - q) <= RADIUS, 0.0, -BIG) for o in (64, 0, 128)], 1)
    kk = np.arange(P)[None, :]
    diag = np.where(q % 2 == kk % 2, 0.0, -BIG)
    edge = np.ones((P, POOL_GROUPS, 16), np.float32)
    for g in range(POOL_GROUPS):
        w = 2 << g
        for c in range(16):
            i = c if c < 8 else T - 16 + c
            edge[:, g, c] = w / (min(i + w // 2, T) - max(i - w // 2, 0))
    return rope, masks.astype(np.float32), diag.astype(np.float32), np.eye(P, dtype=np.float32), edge


WEIGHTS = ("w_in", "pool_maps", "w_up_pool", "w_up_attn", "w_gate", "w_out", "w_ffn_gate", "w_ffn_up",
           "w_ffn_down", "norm_mix", "norm_ffn", "norm_final", "pool_scale", "b_gate")
COLUMNS = ("norm_mix", "norm_ffn", "pool_scale", "b_gate")


def kernel(**inputs):
    import concourse.bacc as bacc
    from concourse.bass_utils import run_bass_kernel_spmd as run

    nc = bacc.Bacc("TRN2", target_bir_lowering=False, num_devices=1)
    arrays = {"x": np.concatenate([np.asarray(inputs["x_prompt"]), np.asarray(inputs["x_sample"])])}
    for name in WEIGHTS:
        a = np.asarray(inputs[name])
        a = a if name == "norm_final" else a[0]
        if name in COLUMNS:
            a = a.reshape(-1, P).T
        arrays[name] = np.ascontiguousarray(a)
    args = [nc.dram_tensor(n, a.shape, F32, kind="ExternalInput").ap() for n, a in arrays.items()]
    consts = [nc.inline_tensor(c, n).ap() for c, n in zip(constants(), ("rope", "masks", "diag", "ident", "edge"))]
    scratch = nc.dram_tensor("records", (2 * GROUPS, T, REC), F32, kind="Internal").ap()
    out = nc.dram_tensor("out", (SEQS, T, D), F32, kind="ExternalOutput").ap()
    encoder(nc, *args, *consts, scratch, out)
    r = run(nc, [arrays], core_ids=[0])
    y = r.results[0]["out"]
    return y[0:1], y[1:2]
```

```python
from contextlib import ExitStack

import numpy as np

import concourse.bass as bass
from concourse import mybir

F32 = mybir.dt.float32
F32R = mybir.dt.float32r
ALU = mybir.AluOpType
ACT = mybir.ActivationFunctionType
AX_X = mybir.AxisListType.X

P = 128
SEQS, T, D = 2, 1024, 1024
KD = D // P
TT = T // P
H2 = 512
HEAD, HPG, GROUPS = 64, 4, 3
DIL = (1, 4, 8)
RADIUS = 64
AW = HEAD * HPG * GROUPS
PW = 512
POOL_GROUPS = 4
FF = 2816
FF_TILES = FF // P
EPS = 1e-6
ROPE_HALF, THETA = 8, 500000.0
REC = 2 * HEAD + 4
UNITS = 2 * TT
BIG = 3.0e38

CREDIT = {"bank_full": 3, "w_ready": 1, "p_ready": 1, "y_sum": 1, "y_ready": 2, "x_added": 8,
          "out_stored": 16}
N_V = (9, 8, 8)
PER_SEQ = {
    "ss_ready": 24, "std_ready": 24, "xn_ready": 16, "hhi_ready": 32, "h_ready": 32,
    "rope_read": 24, "qk_ready": 24, "v_ready": sum(N_V), "s_read": 48, "negmax_ready": 48, "p_ready": 48,
    "pt_ready": 48, "o_ready": 48, "u_ready": 8, "pooled_ready": 4, "pool_hi_ready": 4, "pool_ready": 4,
    "mix_read": 8, "mix_hi_ready": 4, "mixed_ready": 4, "diff_ready": 2, "weight_ready": 2,
    "merged": 2, "mhi_ready": 4, "mT_ready": 4,
    "a_read": 16, "b_read": 16, "sig_ready": 76, "y_sum": 60, "yhi_ready": 60, "y_ready": 60,
    "x_added": 240, "fin_ready": 8, "bias_ready": 8,
}
DMA_SEMS = {"tab_in": 3, "gmix_in": 1, "gffn_in": 1, "gfin_in": 1, "out_stored": 8}
DMA_SEMS.update({f"x_in{t}": 2 for t in range(TT)})
DMA_SEMS.update({"rec_in0": 8, "rec_in1": 8})
DMA_SEMS.update({f"o_stored{n}": 12 for n in range(4)})
PER_SEQ.update(DMA_SEMS)


def due(name, s, n):
    step = 16 if name in DMA_SEMS else 1
    return s * (PER_SEQ[name] * step) + (CREDIT.get(name, 0) + n * step)


def v_tokens(g):
    if g:
        return [(P * j, P) for j in range(TT)]
    return [(RADIUS + P * j, P) for j in range(7)] + [(0, RADIUS), (T - RADIUS, RADIUS)]


def window(g, b):
    if g == 0:
        if b == 0:
            return 0, P + RADIUS, (0, 7), 1
        if b == TT - 1:
            return T - P - RADIUS, P + RADIUS, (6, 8), 0
        return P * b - 64, 256, (b - 1, b), 0
    if g == 1:
        r = b // 2
        return 256 * r, 256, (2 * r, 2 * r + 1), 1 + b % 2
    return P * b, P, (b,), 3


def phase_steps(g):
    if g == GROUPS - 1:
        return [(("u", j), k) for j in reversed(range(8)) for k in range(KD)]
    tiles = [(("proj", g + 1, j), k) for j in range(8) for k in range(KD)]
    values = [(("proj", g + 1, 8 + v), k) for v in range(N_V[g + 1]) for k in range(KD)]
    steps, tiles = tiles[:2 * KD], tiles[2 * KD:]
    for n in range(len(tiles) // 4):
        steps += tiles[4 * n:4 * n + 4] + values[3 * n:3 * n + 3]
    return steps + values[len(tiles) // 4 * 3:]


def cut(g):
    steps = phase_steps(g)
    n_parts = 3 * UNITS if g < GROUPS - 1 else 3 * (UNITS - 2)
    cost = [1 if job[0] == "proj" and job[2] >= 8 else 2 for job, _ in steps]
    total, parts, at_time = sum(cost), [[] for _ in range(3 * UNITS)], 0
    for step, c in zip(steps, cost):
        parts[at_time * n_parts // total].append(step)
        at_time += c
    return parts


PARTS = [p for g in range(GROUPS) for p in cut(g)] + [[], [], []]


def done(first, last):
    return [job for p in PARTS[max(first, 0):last + 1] for job, k in p if k == KD - 1]


LAST = (GROUPS - 1) * UNITS
POOL_DVE = {LAST + 4: [("add", 3, 0, 1)], LAST + 5: [("add", 3, 2, 3)], LAST + 6: [("mean", 3)],
            LAST + 8: [("lo", 3), ("add", 2, 0, 0)], LAST + 9: [("add", 2, 1, 2)], LAST + 10: [("mean", 2)],
            LAST + 11: [("add", 1, 0, 0)], LAST + 12: [("lo", 2), ("add", 1, 1, 1)], LAST + 13: [("mean", 1)],
            LAST + 15: [("lo", 1), ("add", 0, 0, 0)]}
POOL_ACT = {LAST + 7: 3, LAST + 11: 2, LAST + 14: 1}
MIX_ORDER = (1, 3, 2, 0)
for _g, _n in ((3, 9), (2, 13), (1, 16)):
    for _h in range(2):
        PARTS[3 * (LAST + _n) + _h].append((("mix", 2 * _g + _h), KD - 1))



def chunks(g, b):
    lo, wid, tiles, _ = window(g, b)
    at = [v_tokens(g)[v] for v in tiles]
    assert min(at)[0] == lo and sum(n for _, n in at) == wid
    return [(first - lo, n) for first, n in at]


class Plan:

    def __init__(self):
        self.fills = [0] * 8
        self.job, self.before = {}, {}
        self.reader = [("x_added", b + 1 - 8) for b in range(8)]
        self.norm(1)
        for j in range(8 + N_V[0]):
            self.proj(0, j)
        for n in range(GROUPS * UNITS + 1):
            if n < GROUPS * UNITS:
                for h in range(2):
                    self.take(("s", n, h), 4 + h, "s_read", n + 1)
            if n:
                self.take(("pt", n - 1), 6, "pt_ready", n)
                self.take(("o", n - 1), 7, "o_ready", n)
            for part in PARTS[3 * n:3 * n + 3]:
                for job, k in part:
                    if job[0] == "mix":
                        self.mix(job[1])
                    elif k == 0 and job[0] == "proj":
                        self.proj(job[1], job[2])
                    elif k == 0:
                        self.take(job, 1 - job[1] % 2, "u_ready", 8 - job[1])
        for j in range(2):
            self.mix(j)
        for j in range(4):
            self.take(("mt", j), j, "mT_ready", j + 1)
        self.gate0, self.gate_before = list(self.fills), list(self.reader)
        self.fills = [n + GATE_STEPS * GATE_FILLS for n in self.fills]
        self.reader = [("x_added", 16 * GATE_STEPS + b + 1 - 8) for b in range(8)]
        self.norm(2)
        self.ffn0, self.ffn_before = list(self.fills), list(self.reader)
        self.total = [n + FFN_STEPS * FFN_FILLS for n in self.fills]

    def norm(self, which):
        for t in range(TT):
            for half in range(2):
                self.take((f"n{which}", t, half), 4 + 2 * (t % 2) + half, "h_ready",
                          16 * (which - 1) + 2 * t + half + 1)

    def mix(self, j):
        self.take(("mix", j), 2 + j % 2, "mix_read", 2 * (3 - j // 2) + j % 2 + 1)

    def proj(self, g, j):
        if g == 0:
            bank = j if j < 8 else 2 + j % 2
        else:
            bank = j % 2 if j < 8 or j >= 14 else 2 + j % 2
        if j < 8:
            self.take(("proj", g, j), bank, "rope_read", 8 * g + j + 1)
        else:
            self.take(("proj", g, j), bank, "v_ready", sum(N_V[:g]) + j - 8 + 1)

    def take(self, name, bank, sem, count):
        self.fills[bank] += 1
        self.job[name] = (bank, self.fills[bank])
        self.before[name] = self.reader[bank]
        self.reader[bank] = (sem, count)


GATE_STEPS, GATE_FILLS = 4, 4
GATE_FIRST, GATE_NEXT = ("a", "b", "up", "up", "a", "b"), ("up", "a", "b", "up", "a", "b")
GATE_BANK = {"up": 0, "a": 4, "b": 6}
FFN_STEPS, FFN_FILLS = FF_TILES // 2, 3
PLAN = Plan()
CHUNKS = []
for _g in range(GROUPS):
    _q = [(0, ("q", _g, 0), ("proj", _g, 2 if _g == 0 else 1)), (1, ("q", _g, 1), ("proj", _g, 3))]
    _k = [(0, ("k", _g, 0), ("proj", _g, 5)), (1, ("k", _g, 1), ("proj", _g, 7))]
    _v = [(2 + _h, ("v", _g, _h), ("proj", _g, 7 + N_V[_g])) for _h in range(2)]
    CHUNKS += _q + (_k + _v if _g == 0 else _v + _k)
CHUNKS += [(0, ("u", 3), ("u", 6)), (1, ("u", 2), ("u", 4)), (2, ("maps", 1), ("mix", 5)),
           (3, ("maps", 0), ("mix", 1)), (0, ("u", 1), ("u", 2)), (1, ("u", 0), ("u", 0))]
F_PROJ, F_GATE, F_FFN = sum(c[0] == 0 for c in CHUNKS), 3, 2
D_PROJ = sum(c[0] == 2 for c in CHUNKS)
F_TOTAL = F_PROJ + F_GATE * GATE_STEPS + F_FFN * FFN_STEPS
D_TOTAL = D_PROJ + GATE_STEPS + FFN_STEPS
RAW_PROJ = len(CHUNKS) // 2
DVE_STEPS = 129
RAW_TOTAL = RAW_PROJ + 5 * GATE_STEPS + 3 * FFN_STEPS


def order(g, j):
    if g == 0 and j < 4:
        return j % 2, j // 2
    return j // 2, j % 2


class Chain:

    def __init__(self, eng, sem):
        self.eng, self.sem, self.base, self.n = eng, sem, 0, 0

    def link(self, ins):
        self.n += 1
        ins.then_inc(self.sem, 1)
        self.eng.wait_ge(self.sem, self.base + self.n)

    def enter(self, i, per):
        saved = (self.base, self.n)
        self.base, self.n = self.base + self.n + i * per, 0
        return saved

    def leave(self, saved, steps, per):
        assert self.n == per, ("steps in the loop", self.n, per)
        self.base, self.n = saved[0], saved[1] + steps * per


def encoder(nc, x, w_in, maps, w_up_pool, w_up_attn, w_gate, w_out, w_fg, w_fu, w_fd,
            norm_mix, norm_ffn, norm_final, pool_scale, b_gate,
            rope, masks, diag, ident, edge, scratch, out):
    ctx = ExitStack()
    with ctx:
        def sem(name):
            return ctx.enter_context(nc.semaphore(name))

        base = 16512

        def at(name, offset, shape, dt=F32):
            return nc.alloc_sbuf_tensor_at(name, [P] + shape, dt, offset=base + offset)

        h_hi, h_lo = at("h_hi", 0, [KD, T], F32R), at("h_lo", 32768, [KD, T], F32R)
        SLOT = 65536
        w_hi = [at(f"w_hi{s}", SLOT + 8192 * s, [D], F32R) for s in range(4)]
        w_lo = [at(f"w_lo{s}", SLOT + 8192 * s + 4096, [D], F32R) for s in range(4)]
        raw = [at(f"raw{r}", SLOT + 32768 + 4096 * r, [D]) for r in range(2)]
        XR = SLOT + 40960
        X = at("X", XR, [TT, D])
        qk = [at("qk_even", XR, [4, T]), at("qk_odd", XR + 16384, [4, T])]
        U = at("U", XR + 16384, [POOL_GROUPS, T + 16])
        YR = XR + 32768
        y_hi = [at(f"y_hi{j}", YR + 8192 * j, [T], F32R) for j in range(2)]
        y_lo = [at(f"y_lo{j}", YR + 8192 * j + 4096, [T], F32R) for j in range(2)]
        rope_sb = at("rope_sb", YR, [2, T])
        rec = [at("rec0", XR, [4, 6, REC]), at("rec1", YR + 512, [4, 6, REC])]
        masks_sb, diag_sb = at("masks_sb", YR + 8192, [3, 256]), at("diag_sb", YR + 11264, [P])
        MR = YR + 16384
        V = [at("V_even", MR, [11, 256]), at("V_odd", MR + 11264, [8, 256])]
        pool_hi, pool_lo = at("pool_hi", MR + 11264, [T], F32R), at("pool_lo", MR + 15360, [T], F32R)
        masked = at("masked", MR + 19456, [2, 256])
        prob = at("prob", MR + 21504, [2, 2, 256])
        probT = at("probT", MR + 25600, [4, P])
        r_sh, r_c, r_s = (at(f"rope_t{i}", MR + 27648 + 2048 * i, [H2]) for i in range(3))
        o_st = at("o_st", MR + 33792, [4, REC])
        pw0, pw1, pooled = (at("pw0", MR + 35904, [1040]), at("pw1", MR + 40064, [1040]),
                            at("pooled", MR + 44224, [T]))
        mix_hi, mix_lo = at("mix_hi", MR, [4, T], F32R), at("mix_lo", MR + 16384, [4, T], F32R)
        m_hi, m_lo = at("m_hi", MR + 32768, [2, T], F32R), at("m_lo", MR + 40960, [2, T], F32R)
        squares, xn = at("squares", MR, [D]), at("xn", MR + 4096, [2, D])
        gain, g_fin = at("gain", MR + 12288, [D]), at("g_fin", MR + 4096, [D])
        x_first = at("x_first", MR + 16384, [TT, D])
        SR = MR + 49152
        act_t = at("act_t", SR, [3, H2])
        off = [SR + 6144]

        def small(name, shape):
            n = int(np.prod(shape)) * 4
            o = off[0]
            off[0] = o + (n + 31) // 32 * 32
            return at(name, o, shape)

        ident_sb = small("ident_sb", [P])
        p_scale, b_g, edge_sb = small("p_scale", [4]), small("b_g", [16]), small("edge_sb", [4, 16])
        zero, eps, b_now = small("zero", [1]), small("eps", [1]), small("b_now", [2])
        warm = small("warm", [1])
        ss, std, rstd, mx = small("ss", [TT]), small("std", [TT]), small("rstd", [TT]), small("mx", [2])
        mn, den, rden = (at(name, SR + 64 * i, [16]) for i, name in enumerate(("mn", "den", "rden")))
        d3, e3, wd, coef = (at(name, SR + 192 * (i + 1), [3, 16]) for i, name in enumerate(("d3", "e3", "wd", "coef")))
        assert base + off[0] <= nc.sbuf_usable_end
        ps = ctx.enter_context(nc.psum_tensor("ps", [P, 8, H2], F32))

        bank_full = [sem(f"bank_full{b}") for b in range(8)]
        raw_in = [sem(f"raw_in{r}") for r in range(2)]
        w_ready = [sem(f"w_ready{s}") for s in range(4)]
        w_hi_done, zeroed, eps_set, const_in, dve_chain = (
            sem(n) for n in ("w_hi_done", "zeroed", "eps_set", "const_in", "dve_chain"))
        sems = {name: sem(name) for name in PER_SEQ}
        (ss_ready, std_ready, xn_ready, hhi_ready, h_ready, rope_read, qk_ready, v_ready, s_read,
         negmax_ready, p_ready, pt_ready, o_ready, u_ready, pooled_ready, pool_hi_ready, pool_ready, mix_read,
         mix_hi_ready, mixed_ready, diff_ready, weight_ready, merged, mhi_ready, mT_ready, a_read, b_read, sig_ready, y_sum, yhi_ready,
         y_ready, x_added, fin_ready, bias_ready, tab_in, gmix_in, gffn_in, gfin_in, out_stored) = (
            sems[name] for name in PER_SEQ if not name[-1].isdigit())
        x_in = [sems[f"x_in{t}"] for t in range(TT)]
        rec_in = [sems[f"rec_in{t}"] for t in range(2)]
        o_stored = [sems[f"o_stored{t}"] for t in range(4)]

        def filled(s, b, n):
            return s * PLAN.total[b] + (CREDIT["bank_full"] + n)

        def split_by(s, slot, n):
            return s * (F_TOTAL if slot < 2 else D_TOTAL) + (CREDIT["w_ready"] + n)

        x_t = x.rearrange("s (t p) d -> s t p d", p=P)
        out_t = out.rearrange("s (t p) d -> s t p d", p=P)
        block = ctx.enter_context(nc.Block())

        @block.sync
        def _(sp):
            def cols(w):
                return w.rearrange("(k p) c -> p k c", p=P)

            w_in_c, w_gate_c = cols(w_in), cols(w_gate)
            upp_c, upa_c, fg_c, fu_c = cols(w_up_pool), cols(w_up_attn), cols(w_fg), cols(w_fu)
            w_out_r = w_out.rearrange("(k p) c -> k p c", p=P)
            w_fd_r = w_fd.rearrange("(k p) c -> k p c", p=P)
            maps_c = maps.rearrange("g c d -> c g d")

            def r3(r, n):
                return raw[r][:, 0:n * P].rearrange("p (k c) -> p k c", c=P)

            def raws_free(s, i, r):
                cols_split = sp.snap(s * F_TOTAL + (i * F_GATE + (F_PROJ + 1)))
                rows_split = sp.snap(s * D_TOTAL + (i + (D_PROJ + 1)))
                sp.wait_ge(w_ready[r], cols_split)
                sp.wait_ge(w_ready[2 + r], rows_split)

            def load_x(s, tiles):
                for t in tiles:
                    sp.dma_start(x_first[:, t, :], x_t[s, t]).then_inc(x_in[t], 16)

            def load_records(s, q0, q1):
                for t in range(TT):
                    sp.dma_start(rec[t // 4][:, t % 4, q0:q1, :],
                                 scratch[q0:q1, t * P:(t + 1) * P, :].rearrange("q t c -> t q c")
                                 ).then_inc(rec_in[t // 4], 16)

            def gate_chunks(s, i, kinds):
                for n, kind in enumerate(kinds):
                    j, r = n // 3, n % 2
                    if n < 2:
                        raws_free(s, i, r)
                    else:
                        sp.wait_ge(w_ready[r], split_by(s, r, i * F_GATE + (F_PROJ + n // 2)))
                    if kind == "up":
                        col = bass.ds(i * 256 + P * j, P)
                        sp.dma_start(r3(r, 4), upp_c[:, :, col]).then_inc(raw_in[r], 16)
                        sp.dma_start(raw[r][:, 4 * P:6 * P].rearrange("p (k c) -> p k c", c=P),
                                     upa_c[:, :, col]).then_inc(raw_in[r], 16)
                    else:
                        col = bass.ds(i * 256 + (P * j + (D if kind == "b" else 0)), P)
                        sp.dma_start(r3(r, 8), w_gate_c[:, :, col]).then_inc(raw_in[r], 16)
                    if n == 1 and kinds is GATE_FIRST:
                        scores_read = sp.snap(due("s_read", s, GROUPS * UNITS))
                        sp.wait_ge(s_read, scores_read)
                        load_records(s, 0, 4)
                        for q in range(4):
                            stored = sp.snap(due(f"o_stored{q}", s, 12))
                            sp.wait_ge(o_stored[q], stored)
                        load_records(s, 4, 6)
                if kinds is GATE_FIRST:
                    u_read = sp.snap(due("mixed_ready", s, POOL_GROUPS))
                    sp.wait_ge(mixed_ready, u_read)
                    records_read = sp.snap(due("mT_ready", s, 4))
                    sp.wait_ge(mT_ready, records_read)
                    for t in range(TT):
                        sp.dma_start(X[:, t, :], x_t[s, t]).then_inc(x_in[t], 16)
                for j in range(2):
                    sp.wait_ge(w_ready[j], split_by(s, j, i * F_GATE + (F_PROJ + 3)))
                    sp.dma_start(raw[j][:, :], w_out_r[i * 2 + j]).then_inc(raw_in[j], 16)

            with sp.Fori(0, SEQS) as s:
                done = [0] * 4
                load_x(s, [0])
                sp.dma_start(gain[:, :], norm_mix.partition_broadcast(P)).then_inc(gmix_in, 16)
                load_x(s, [1])
                for c, (slot, what, _) in enumerate(CHUNKS):
                    r, kind = c % 2, what[0]
                    if c == 1:
                        load_x(s, [2])
                    if c == 2:
                        load_x(s, range(3, TT))
                        y_used = sp.snap(due("x_added", s, 0))
                        sp.wait_ge(x_added, y_used)
                        for dst, src in ((rope_sb[:, :, :], rope), (masks_sb[:, :, :], masks), (diag_sb[:, :], diag)):
                            sp.dma_start(dst, src).then_inc(tab_in, 16)
                    if c < 2:
                        sp.wait_ge(w_ready[2 + c], split_by(s, 2 + c, 0))
                    else:
                        before = CHUNKS[c - 2][0]
                        sp.wait_ge(w_ready[before], split_by(s, before, done[before]))
                    done[slot] += 1
                    if kind == "u":
                        src, dst = w_in_c[:, :, P * what[1]:P * what[1] + P], r3(r, 8)
                    elif kind == "maps":
                        src, dst = maps_c[:, 2 * what[1]:2 * what[1] + 2, :], r3(r, 2)
                    elif kind == "v":
                        at_c = PW + 2 * AW + 256 * what[1]
                        src = w_in_c[:, 4 * what[2]:4 * what[2] + 4, at_c:at_c + 256]
                        dst = raw[r][:, :].rearrange("p (k c) -> p k c", c=256)
                    else:
                        at_c = PW + (AW if kind == "k" else 0) + 256 * what[1] + P * what[2]
                        src, dst = w_in_c[:, :, at_c:at_c + P], r3(r, 8)
                    sp.dma_start(dst, src).then_inc(raw_in[r], 16)
                gate_chunks(s, 0, GATE_FIRST)
                with sp.Fori(1, GATE_STEPS) as i:
                    gate_chunks(s, i, GATE_NEXT)
                f0 = F_PROJ + GATE_STEPS * F_GATE
                with sp.Fori(0, FFN_STEPS) as i:
                    for j in range(2):
                        col = bass.ds(i * 256 + P * j, P)
                        for k, w in enumerate((fg_c, fu_c)):
                            if j == 0:
                                sp.wait_ge(w_ready[2 + k], s * D_TOTAL + i + (1 + D_PROJ + GATE_STEPS))
                            else:
                                sp.wait_ge(w_ready[k], split_by(s, k, f0 + i * F_FFN + 1))
                            sp.dma_start(r3(k, 8), w[:, :, col]).then_inc(raw_in[k], 16)
                    for j in range(2):
                        sp.wait_ge(w_ready[j], split_by(s, j, f0 + i * F_FFN + 2))
                        sp.dma_start(raw[j][:, :], w_fd_r[i * 2 + j]).then_inc(raw_in[j], 16)

        @block.gpsimd
        def _(pool):
            chain = Chain(pool, w_hi_done)
            for s4 in range(4):
                pool.sem_inc(w_ready[s4], 1)
            nc.gpsimd.memset(zero[:, :], 0.0).then_inc(zeroed, 1)
            pool.wait_ge(zeroed, 1)

            def split(s, r, n_raw, slot, width=D):
                pool.wait_ge(raw_in[r], (s * RAW_TOTAL + n_raw) * 16)
                chain.link(nc.gpsimd.tensor_tensor(w_hi[slot][:, 0:width], raw[r][:, 0:width],
                                                   zero[:, :].broadcast_to([P, width]), ALU.add))
                nc.gpsimd.tensor_tensor(w_lo[slot][:, 0:width], raw[r][:, 0:width],
                                        w_hi[slot][:, 0:width].bitcast(F32), ALU.subtract
                                        ).then_inc(w_ready[slot], 1)

            def gate_splits(s, i, kinds):
                def gate_use(b, n):
                    pool.wait_ge(bank_full[b], filled(s, b, i * GATE_FILLS + (PLAN.gate0[b] + n)))

                def used(job):
                    b, n = PLAN.job[job]
                    pool.wait_ge(bank_full[b], filled(s, b, n))

                raw_n = [0, 0]
                for n, kind in enumerate(kinds):
                    r = n % 2
                    raw_n[r] += 2 if kind == "up" else 1
                    if n >= 2:
                        gate_use(GATE_BANK[kinds[n - 2]] + (3 if kinds[n - 2] == "up" else 1), (n - 2) // 3 + 1)
                    elif kinds is GATE_FIRST:
                        used(("u", 2 - 2 * n))
                    else:
                        gate_use(5 + 2 * n, -2)
                    split(s, r, i * 5 + (RAW_PROJ + raw_n[r]), r, 6 * P if kind == "up" else D)
                    if n == 1 and kinds is GATE_FIRST:
                        for m, g in enumerate(MIX_ORDER):
                            pool.wait_ge(mix_hi_ready, due("mix_hi_ready", s, m + 1))
                            nc.gpsimd.tensor_tensor(mix_lo[:, g, :], U[:, g, 8:8 + T], mix_hi[:, g, :].bitcast(F32),
                                                    ALU.subtract).then_inc(mixed_ready, 1)
                gate_use(0, 0)
                split(s, 0, i * 5 + (RAW_PROJ + 5), 2)
                if kinds is GATE_FIRST:
                    used(("mix", 1))
                gate_use(7, 0)
                split(s, 1, i * 5 + (RAW_PROJ + 5), 3)

            def ffn_splits(s, i, first):
                def ffn_use(b, n):
                    pool.wait_ge(bank_full[b], filled(s, b, i * FFN_FILLS + (PLAN.ffn0[b] + n)))

                r0 = RAW_PROJ + GATE_STEPS * 5 + i * 3
                if first:
                    pool.wait_ge(bank_full[5], filled(s, 5, PLAN.gate0[5] + GATE_STEPS * GATE_FILLS - 2))
                else:
                    ffn_use(5, -2)
                split(s, 0, r0 + 1, 0)
                if first:
                    pool.wait_ge(bank_full[7], filled(s, 7, PLAN.gate0[7] + GATE_STEPS * GATE_FILLS - 2))
                else:
                    ffn_use(7, -2)
                split(s, 1, r0 + 1, 1)
                ffn_use(1, 1)
                split(s, 0, r0 + 2, 0)
                ffn_use(3, 1)
                split(s, 1, r0 + 2, 1)
                ffn_use(0, 0)
                split(s, 0, r0 + 3, 2)
                ffn_use(7, 0)
                split(s, 1, r0 + 3, 3)

            SPLITS = len(CHUNKS) + 8 * GATE_STEPS + 6 * FFN_STEPS
            with pool.Fori(0, SEQS) as s:
                saved = chain.enter(s, SPLITS)
                last_use = {}
                for c, (slot, what, job) in enumerate(CHUNKS):
                    if slot in last_use:
                        b, n = PLAN.job[last_use[slot]]
                        pool.wait_ge(bank_full[b], filled(s, b, n))
                    else:
                        b, n = ((5, -2), (7, -2), (0, 0), (7, 0))[slot]
                        pool.wait_ge(bank_full[b], filled(s, b, n))
                    last_use[slot] = job
                    split(s, c % 2, c // 2 + 1, slot, 2 * P if what[0] == "maps" else D)
                gate_splits(s, 0, GATE_FIRST)
                with pool.Fori(1, GATE_STEPS) as i:
                    inner = chain.enter(i - 1, 8)
                    gate_splits(s, i, GATE_NEXT)
                    chain.leave(inner, GATE_STEPS - 1, 8)
                ffn_splits(s, 0, True)
                with pool.Fori(1, FFN_STEPS) as i:
                    inner = chain.enter(i - 1, 6)
                    ffn_splits(s, i, False)
                    chain.leave(inner, FFN_STEPS - 1, 6)
                chain.leave(saved, SEQS, SPLITS)

        @block.tensor
        def _(pe):
            for b in range(8):
                pe.sem_inc(bank_full[b], CREDIT["bank_full"])
            pe.wait_ge(const_in, 16 * 4)

            def col_job(bank, slot, half, ks, first, last, rhs=(h_hi, h_lo), w0=0, quarter=None):
                q0, n = (0, H2) if quarter is None else (quarter * H2 // 2, H2 // 2)
                o = ps[:, bank, q0:q0 + n]
                for k in ks:
                    wh = w_hi[slot][:, (w0 + k) * P:(w0 + k + 1) * P]
                    wl = w_lo[slot][:, (w0 + k) * P:(w0 + k + 1) * P]
                    rh, rl = (r[:, k, half * H2 + q0:half * H2 + q0 + n] for r in rhs)
                    nc.tensor.matmul(o, wh, rh, start=(k == first), stop=False)
                    nc.tensor.matmul(o, wh, rl, start=False, stop=False)
                    ins = nc.tensor.matmul(o, wl, rh, start=False, stop=(k == last))
                if ks[-1] == last and quarter != 0:
                    ins.then_inc(bank_full[bank], 1)

            def perm(hx, k, g, first, length):
                d, n = DIL[g], T // DIL[g]
                return hx[:, k, :].rearrange("p (i r) -> p r i", r=d)[:, first // n, first % n:first % n + length]

            def v_job(bank, g, v, ks):
                first, length = v_tokens(g)[v]
                o = ps[0:length, bank, 0:256]
                for k in ks:
                    slot, kk = 2 + k // 4, k % 4
                    rh = w_hi[slot][:, kk * 256:(kk + 1) * 256]
                    rl = w_lo[slot][:, kk * 256:(kk + 1) * 256]
                    lh, ll = perm(h_hi, k, g, first, length), perm(h_lo, k, g, first, length)
                    nc.tensor.matmul(o, lh, rh, start=(k == 0), stop=False)
                    nc.tensor.matmul(o, lh, rl, start=False, stop=False)
                    ins = nc.tensor.matmul(o, ll, rh, start=False, stop=(k == KD - 1))
                if ks[-1] == KD - 1:
                    ins.then_inc(bank_full[bank], 1)

            def proj_steps(s, job, ks):
                j, bank = job[-1], PLAN.job[job][0]
                if ks[0] == 0:
                    reader, n = PLAN.before[job]
                    pe.wait_ge(sems[reader], due(reader, s, n))
                if job[0] == "u":
                    tile, half, chunks = 3 - j // 2, j % 2, 2 * GROUPS
                    begins = half == 1
                elif j < 8:
                    (tile, half), chunks = order(job[1], j), 2 * job[1]
                    begins = half == 0
                else:
                    if ks[0] == 0:
                        pe.wait_ge(w_ready[2], split_by(s, 2, job[1] + 1))
                        pe.wait_ge(w_ready[3], split_by(s, 3, job[1] + 1))
                    v_job(bank, job[1], j - 8, ks)
                    return
                if ks[0] == 0 and begins:
                    pe.wait_ge(w_ready[tile % 2], split_by(s, tile % 2, chunks + tile // 2 + 1))
                col_job(bank, tile % 2, half, ks, 0, KD - 1)

            def projections(s, part):
                for job, k in PARTS[part]:
                    if job[0] == "mix":
                        mix_job(s, job[1])
                    else:
                        proj_steps(s, job, [k])

            def mix_job(s, j):
                g, half = j // 2, j % 2
                b = PLAN.job["mix", j][0]
                reader, n = PLAN.before["mix", j]
                pe.wait_ge(sems[reader], due(reader, s, n))
                slot = 3 - g // 2
                if half == 0:
                    pe.wait_ge(pool_ready, due("pool_ready", s, POOL_GROUPS - g))
                    if g % 2:
                        pe.wait_ge(w_ready[slot], split_by(s, slot, D_PROJ))
                o, m = ps[:, b, :], slice((g % 2) * P, (g % 2 + 1) * P)
                tok = slice(half * H2, (half + 1) * H2)
                nc.tensor.matmul(o, w_hi[slot][:, m], pool_hi[:, tok], start=True, stop=False)
                nc.tensor.matmul(o, w_hi[slot][:, m], pool_lo[:, tok], start=False, stop=False)
                nc.tensor.matmul(o, w_lo[slot][:, m], pool_hi[:, tok], start=False, stop=True
                                 ).then_inc(bank_full[b], 1)

            def norm_transposes(s, which, tiles):
                for t in tiles:
                    pe.wait_ge(xn_ready, due("xn_ready", s, 8 * (which - 1) + t + 1))
                    for half in range(2):
                        b = PLAN.job[f"n{which}", t, half][0]
                        reader, n = PLAN.before[f"n{which}", t, half]
                        pe.wait_ge(sems[reader], due(reader, s, n))
                        for k in range(4):
                            c = (4 * half + k) * P
                            ins = nc.tensor.transpose(ps[:, b, k * P:(k + 1) * P], xn[:, t % 2, c:c + P],
                                                      ident_sb[:, :])
                        ins.then_inc(bank_full[b], 1)

            def normed(s, which, product):
                norm_transposes(s, which, range(3))
                for a, quarter in ((0, 0), (1, 0), (0, 1), (1, 1), (0, 2), (0, 3), (1, 2), (1, 3)):
                    pe.wait_ge(h_ready, due("h_ready", s, 16 * (which - 1) + 4 * (quarter + 1)))
                    product(s, a, quarter)
                    tiles = {(0, 0): [3], (1, 0): [4], (0, 1): [5], (1, 1): [6, 7]}
                    norm_transposes(s, which, tiles.get((a, quarter), []))

            def first_queries(s, a, quarter):
                job = ("proj", 0, a + 2 * (quarter // 2))
                bank = PLAN.job[job][0]
                if quarter == 0:
                    pe.wait_ge(w_ready[a], split_by(s, a, 1))
                if quarter % 2 == 0:
                    reader, n = PLAN.before[job]
                    pe.wait_ge(sems[reader], due(reader, s, n))
                col_job(bank, a, quarter // 2, range(KD), 0, KD - 1, quarter=quarter % 2)

            def first_hidden(s, a, quarter):
                bank = 2 * a + quarter // 2
                if quarter == 0:
                    pe.wait_ge(w_ready[a], split_by(s, a, F_PROJ + GATE_STEPS * F_GATE + 1))
                if quarter % 2 == 0:
                    reader, n = PLAN.ffn_before[bank]
                    pe.wait_ge(sems[reader], due(reader, s, n))
                col_job(bank, a, quarter // 2, range(KD), 0, KD - 1, quarter=quarter % 2)

            def scores(s, unit):
                g, u = unit // UNITS, unit % UNITS
                pair, b = u // TT, u % TT
                lo, wid, _, _ = window(g, b)
                if u == 0:
                    pe.wait_ge(qk_ready, due("qk_ready", s, 8 * (g + 1)))
                for h in range(2):
                    bank = PLAN.job["s", unit, h][0]
                    reader, n = PLAN.before["s", unit, h]
                    pe.wait_ge(sems[reader], due(reader, s, n))
                    rows = slice(HEAD * h, HEAD * h + HEAD)
                    nc.tensor.matmul(ps[:, bank, 0:wid], qk[g % 2][rows, pair, b * P:(b + 1) * P],
                                     qk[g % 2][rows, 2 + pair, lo:lo + wid], start=True, stop=True
                                     ).then_inc(bank_full[bank], 1)

            def prob_transposes(s, unit):
                g, u = unit // UNITS, unit % UNITS
                pe.wait_ge(p_ready, due("p_ready", s, unit + 1))
                bank = PLAN.job["pt", unit][0]
                reader, n = PLAN.before["pt", unit]
                pe.wait_ge(sems[reader], due(reader, s, n))
                n = 0
                for h in range(2):
                    for first, length in chunks(g, u % TT):
                        ins = nc.tensor.transpose(ps[0:length, bank, n * P:(n + 1) * P],
                                                  prob[:, u % 2, h, first:first + length], ident_sb[:, :])
                        n += 1
                ins.then_inc(bank_full[bank], 1)

            def prob_v(s, unit):
                g, u = unit // UNITS, unit % UNITS
                pair = u // TT
                tiles = window(g, u % TT)[2]
                if u == 0:
                    pe.wait_ge(v_ready, due("v_ready", s, sum(N_V[:g + 1])))
                pe.wait_ge(pt_ready, due("pt_ready", s, unit + 1))
                bank = PLAN.job["o", unit][0]
                reader, n = PLAN.before["o", unit]
                pe.wait_ge(sems[reader], due(reader, s, n))
                n = 0
                for h in range(2):
                    e = (2 * pair + h) * HEAD
                    for c, v in enumerate(tiles):
                        length = v_tokens(g)[v][1]
                        ins = nc.tensor.matmul(ps[:, bank, h * HEAD:(h + 1) * HEAD], probT[0:length, n, :],
                                               V[g % 2][0:length, v, e:e + HEAD], start=(c == 0),
                                               stop=(c == len(tiles) - 1))
                        n += 1
                ins.then_inc(bank_full[bank], 1)

            def row_step(s, n_w, n_y, n_x, reader):
                for rnd in range(2):
                    for j in range(2):
                        if rnd == 0:
                            pe.wait_ge(w_ready[2 + j], split_by(s, 2 + j, n_w))
                            pe.wait_ge(y_ready, due("y_ready", s, n_y + 2 * j + 2))
                        for b in range(8):
                            t, n = (8 * rnd + b) // 2, b % 2
                            if j == 0 and rnd == 0:
                                pe.wait_ge(sems[reader[b][0]], due(reader[b][0], s, reader[b][1]))
                            elif j == 0:
                                pe.wait_ge(x_added, due("x_added", s, n_x + b + 1))
                            o = ps[:, b, :]
                            tok, col = slice(t * P, (t + 1) * P), slice(n * H2, (n + 1) * H2)
                            nc.tensor.matmul(o, y_hi[j][:, tok], w_hi[2 + j][:, col], start=(j == 0), stop=False)
                            nc.tensor.matmul(o, y_hi[j][:, tok], w_lo[2 + j][:, col], start=False, stop=False)
                            ins = nc.tensor.matmul(o, y_lo[j][:, tok], w_hi[2 + j][:, col],
                                                   start=False, stop=(j == 1))
                            if j == 1:
                                ins.then_inc(bank_full[b], 1)

            def merged_transposes(s):
                for batch in range(2):
                    pe.wait_ge(merged, due("merged", s, batch + 1))
                    for pair in range(2):
                        job = ("mt", 2 * batch + pair)
                        b = PLAN.job[job][0]
                        reader, n = PLAN.before[job]
                        pe.wait_ge(sems[reader], due(reader, s, n))
                        for t in range(4):
                            ins = nc.tensor.transpose(ps[:, b, t * P:(t + 1) * P],
                                                      rec[batch][:, t, pair, 0:2 * HEAD], ident_sb[:, :])
                        ins.then_inc(bank_full[b], 1)

            def gate_step(s, i, kinds):
                first = kinds is GATE_FIRST
                for n, kind in enumerate(kinds):
                    j, slot = n // 3, n % 2
                    f = i * 2 + (j - 1)

                    def bank_read(b, name, count):
                        if j == 1:
                            pe.wait_ge(sems[name], due(name, s, count))
                        elif first:
                            reader, before = PLAN.gate_before[b]
                            pe.wait_ge(sems[reader], due(reader, s, before))
                        else:
                            pe.wait_ge(x_added, due("x_added", s, i * 16 + (b + 1 - 8)))

                    if first and n == 2:
                        merged_transposes(s)
                        pe.wait_ge(mixed_ready, due("mixed_ready", s, POOL_GROUPS))
                    pe.wait_ge(w_ready[slot], split_by(s, slot, i * F_GATE + (F_PROJ + n // 2 + 1)))
                    for half in range(2):
                        b = GATE_BANK[kind] + half
                        if kind == "up":
                            bank_read(b, "a_read", f * 2 + (half + 1))
                            col_job(b, slot, half, range(4), 0, 3, (mix_hi, mix_lo))
                        else:
                            bank_read(b, "sig_ready", f * 4 + ((2 if kind == "b" else 0) + half + 1))
                            col_job(b, slot, half, range(KD), 0, KD - 1)
                            if first and n + half == 0:
                                mix_job(s, 0)
                                mix_job(s, 1)
                    if kind == "up":
                        if first and j == 0:
                            pe.wait_ge(mT_ready, due("mT_ready", s, 4))
                        for half in range(2):
                            bank_read(2 + half, "b_read", f * 2 + (half + 1))
                            col_job(2 + half, slot, half, range(2), 0, 1, (m_hi, m_lo), 4)
                last = i * 2 + 1
                reader = ([(name, last * 2 + (half + 1)) for name in ("a_read", "b_read") for half in range(2)]
                          + [("sig_ready", last * 4 + (n + 1)) for n in range(4)])
                row_step(s, i + (D_PROJ + 1), i * 4, i * 16, reader)

            def ffn_step(s, i, first):
                for j in range(1 if first else 0, 2):
                    for c in range(2):
                        pe.wait_ge(w_ready[c], split_by(s, c, i * F_FFN + (F_PROJ + GATE_STEPS * F_GATE + j + 1)))
                        for half in range(2):
                            b = 4 * j + 2 * c + half
                            if first:
                                before, n = PLAN.ffn_before[b]
                                pe.wait_ge(sems[before], due(before, s, n))
                            else:
                                pe.wait_ge(x_added, due("x_added", s, i * 16 + (16 * GATE_STEPS + b + 1 - 8)))
                            col_job(b, c, half, range(KD), 0, KD - 1)
                reader = [("sig_ready" if (b // 2) % 2 == 0 else "y_sum",
                           i * 4 + ((32 if (b // 2) % 2 == 0 else 16) + 2 * (b // 4) + b % 2 + 1)) for b in range(8)]
                row_step(s, i + (D_PROJ + GATE_STEPS + 1), i * 4 + 16, i * 16 + 16 * GATE_STEPS, reader)

            with pe.Fori(0, SEQS) as s:
                normed(s, 1, first_queries)
                for j in range(4, 8 + N_V[0]):
                    proj_steps(s, ("proj", 0, j), range(KD))
                for unit in range(GROUPS * UNITS + 1):
                    busy = unit < GROUPS * UNITS
                    if busy:
                        scores(s, unit)
                    projections(s, 3 * unit)
                    if unit:
                        prob_transposes(s, unit - 1)
                    projections(s, 3 * unit + 1)
                    if unit:
                        prob_v(s, unit - 1)
                    projections(s, 3 * unit + 2)
                gate_step(s, 0, GATE_FIRST)
                with pe.Fori(1, GATE_STEPS) as i:
                    gate_step(s, i, GATE_NEXT)
                normed(s, 2, first_hidden)
                ffn_step(s, 0, True)
                with pe.Fori(1, FFN_STEPS) as i:
                    ffn_step(s, i, False)

        @block.scalar
        def _(act):
            act.sem_inc(p_ready, CREDIT["p_ready"])
            act.sem_inc(out_stored, CREDIT["out_stored"])
            for dst, src in ((ident_sb[:, :], ident), (p_scale[:, :], pool_scale), (b_g[:, :], b_gate),
                             (edge_sb[:, :, :], edge)):
                act.dma_start(dst, src).then_inc(const_in, 16)
            act.wait_ge(eps_set, 1)

            def stats(s, n, t, x_now=X):
                nc.scalar.activation(squares[:, :], x_now[:, t, :], ACT.Square, accum_out=ss[:, t:t + 1]
                                     ).then_inc(ss_ready, 1)
                act.wait_ge(ss_ready, due("ss_ready", s, n))
                nc.scalar.activation(std[:, t:t + 1], ss[:, t:t + 1], ACT.Sqrt,
                                     bias=eps[:, :], scale=1.0 / D).then_inc(std_ready, 1)

            def round_h(s, which, t):
                for half in range(2):
                    b, n = PLAN.job[f"n{which}", t, half]
                    act.wait_ge(bank_full[b], filled(s, b, n))
                    nc.scalar.copy(h_hi[:, 4 * half:4 * half + 4, t * P:(t + 1) * P],
                                   ps[:, b, :].rearrange("p (k q) -> p k q", q=P)).then_inc(hhi_ready, 1)

            def evict_v(s, g, v):
                b, n = PLAN.job["proj", g, 8 + v]
                act.wait_ge(bank_full[b], filled(s, b, n))
                length = v_tokens(g)[v][1]
                nc.scalar.copy(V[g % 2][0:length, v, :], ps[0:length, b, 0:256]).then_inc(v_ready, 1)

            def exp_unit(s, unit):
                wid = window(unit // UNITS, unit % TT)[1]
                act.wait_ge(negmax_ready, due("negmax_ready", s, unit + 1))
                for h in range(2):
                    ins = nc.scalar.activation(prob[:, unit % 2, h, 0:wid], masked[:, h, 0:wid], ACT.Exp,
                                               bias=o_st[:, unit % 4, 2 * HEAD + h:2 * HEAD + h + 1],
                                               scale=HEAD ** -0.5,
                                               accum_out=o_st[:, unit % 4, 2 * HEAD + 2 + h:2 * HEAD + 3 + h])
                ins.then_inc(p_ready, 1)

            def evict_probs(s, unit):
                lengths = [length for _, length in chunks(unit // UNITS, unit % TT)]
                n_c = len(lengths)
                b, n = PLAN.job["pt", unit]
                act.wait_ge(bank_full[b], filled(s, b, n))
                if lengths[0] == lengths[-1]:
                    ins = nc.scalar.copy(probT[:, 0:2 * n_c, :],
                                         ps[:, b, 0:2 * n_c * P].rearrange("p (n q) -> p n q", q=P))
                else:
                    for c, length in enumerate(lengths):
                        ins = nc.scalar.copy(probT[0:length, c:c + n_c + 1:n_c, :],
                                             ps[0:length, b, :].rearrange("p (n q) -> p n q", q=P)[:, c:c + n_c + 1:n_c, :])
                ins.then_inc(pt_ready, 1)

            def evict_unit(s, unit):
                g, u = unit // UNITS, unit % UNITS
                b, n = PLAN.job["o", unit]
                act.wait_ge(bank_full[b], filled(s, b, n))
                nc.scalar.copy(o_st[:, u % 4, 0:2 * HEAD], ps[:, b, 0:2 * HEAD]).then_inc(o_ready, 1)
                act.wait_ge(o_ready, due("o_ready", s, unit + 1))
                pair, qb = u // TT, u % TT
                by_res = scratch[2 * g + pair].rearrange("(i r) c -> r i c", r=DIL[g])
                n = T // DIL[g] // P
                act.dma_start(by_res[qb // n, (qb % n) * P:(qb % n + 1) * P, :], o_st[:, u % 4, :]
                              ).then_inc(o_stored[u % 4], 16)

            def evict_mix(s, j):
                g, half = j // 2, j % 2
                b, n = PLAN.job["mix", j]
                act.wait_ge(bank_full[b], filled(s, b, n))
                nc.scalar.activation(U[:, g, 8 + half * H2:8 + (half + 1) * H2], ps[:, b, :], ACT.Identity,
                                     scale=p_scale[:, g:g + 1]).then_inc(mix_read, 1)

            def round_pooled(s, g):
                act.wait_ge(pooled_ready, due("pooled_ready", s, POOL_GROUPS - g))
                nc.scalar.copy(pool_hi[:, :], pooled[:, :]).then_inc(pool_hi_ready, 1)

            with act.Fori(0, SEQS) as s:
                nc.scalar.activation(warm[:, :], eps[:, :], ACT.Sqrt)
                for t in range(TT + 1):
                    if t < TT:
                        act.wait_ge(x_in[t], due(f"x_in{t}", s, 1))
                        stats(s, t + 1, t, x_first)
                    if t:
                        round_h(s, 1, t - 1)
                act.wait_ge(const_in, 16 * 4)
                for v in range(N_V[0]):
                    evict_v(s, 0, v)
                for unit in range(GROUPS * UNITS + 1):
                    if unit:
                        evict_probs(s, unit - 1)
                    if unit < GROUPS * UNITS:
                        exp_unit(s, unit)
                    if unit:
                        evict_unit(s, unit - 1)
                        for job in done(3 * unit - 1, 3 * unit + 1):
                            if job[0] == "u":
                                b, n = PLAN.job[job]
                                j = job[1]
                                act.wait_ge(bank_full[b], filled(s, b, n))
                                nc.scalar.copy(U[:, j // 2, 8 + (j % 2) * H2:8 + (j % 2 + 1) * H2], ps[:, b, :]
                                               ).then_inc(u_ready, 1)
                            elif job[0] == "mix":
                                evict_mix(s, job[1])
                            elif job[2] >= 8:
                                evict_v(s, job[1], job[2] - 8)
                    if unit in POOL_ACT:
                        round_pooled(s, POOL_ACT[unit])
                round_pooled(s, 0)

                def round_mix(g):
                    act.wait_ge(mix_read, due("mix_read", s, 6 if g == MIX_ORDER[0] else 8))
                    nc.scalar.copy(mix_hi[:, g, :], U[:, g, 8:8 + T]).then_inc(mix_hi_ready, 1)

                round_mix(MIX_ORDER[0])
                for batch in range(2):
                    act.wait_ge(diff_ready, due("diff_ready", s, batch + 1))
                    nc.scalar.activation(e3[:, :, :], d3[:, :, :], ACT.Exp).then_inc(weight_ready, 1)
                    if batch == 0:
                        for half in range(2):
                            evict_mix(s, half)
                        for g in MIX_ORDER[1:]:
                            round_mix(g)
                for j in range(4):
                    b, n = PLAN.job["mt", j]
                    act.wait_ge(bank_full[b], filled(s, b, n))
                    nc.scalar.copy(m_hi[:, j % 2, (j // 2) * H2:(j // 2 + 1) * H2], ps[:, b, :]
                                   ).then_inc(mhi_ready, 1)
                with act.Fori(0, GATE_STEPS) as i:
                    for j in range(2):
                        f = i * 2 + j
                        nc.scalar.copy(b_now[:, :], b_g[:, :].rearrange("p (g f) -> p f g", g=2)[:, bass.ds(f, 1), :]
                                       .rearrange("p a g -> p (a g)")).then_inc(bias_ready, 1)
                        act.wait_ge(bias_ready, due("bias_ready", s, f + 1))
                        for half in range(2):
                            act.wait_ge(bank_full[4 + half], filled(s, 4 + half, i * GATE_FILLS + (PLAN.gate0[4 + half] + j + 1)))
                            act.wait_ge(y_ready, due("y_ready", s, f * 2 + (half - 1)))
                            nc.scalar.activation(act_t[:, half, :], ps[:, 4 + half, :], ACT.Sigmoid,
                                                 bias=b_now[:, 0:1]).then_inc(sig_ready, 1)
                        for half in range(2):
                            act.wait_ge(bank_full[6 + half], filled(s, 6 + half, i * GATE_FILLS + (PLAN.gate0[6 + half] + j + 1)))
                            act.wait_ge(y_sum, due("y_sum", s, f * 2 + half))
                            nc.scalar.activation(act_t[:, 2, :], ps[:, 6 + half, :], ACT.Sigmoid,
                                                 bias=b_now[:, 1:2]).then_inc(sig_ready, 1)
                            act.wait_ge(y_sum, due("y_sum", s, f * 2 + (half + 1)))
                            nc.scalar.copy(y_hi[j][:, half * H2:(half + 1) * H2], act_t[:, half, :]
                                           ).then_inc(yhi_ready, 1)
                act.dma_start(gain[:, :], norm_ffn.partition_broadcast(P)).then_inc(gffn_in, 16)
                for t in range(TT + 1):
                    if t < TT:
                        act.wait_ge(x_added, due("x_added", s, 16 * GATE_STEPS - 16 + 2 * (t + 1)))
                        stats(s, TT + t + 1, t)
                    if t:
                        round_h(s, 2, t - 1)
                act.dma_start(g_fin[:, :], norm_final.partition_broadcast(P)).then_inc(gfin_in, 16)
                with act.Fori(0, FFN_STEPS) as i:
                    for j in range(2):
                        n = i * 4 + (16 + 2 * j)
                        for half in range(2):
                            act.wait_ge(bank_full[4 * j + half], filled(s, 4 * j + half, i * FFN_FILLS + (PLAN.ffn0[4 * j + half] + 1)))
                            act.wait_ge(y_ready, due("y_ready", s, n + (half - 1)))
                            nc.scalar.activation(act_t[:, half, :], ps[:, 4 * j + half, :], ACT.Silu
                                                 ).then_inc(sig_ready, 1)
                        for half in range(2):
                            act.wait_ge(y_sum, due("y_sum", s, n + (half + 1)))
                            nc.scalar.copy(y_hi[j][:, half * H2:(half + 1) * H2], act_t[:, half, :]
                                           ).then_inc(yhi_ready, 1)
                for rnd in range(2):
                    for t in range(4 * rnd, 4 * rnd + 4):
                        act.wait_ge(x_added, due("x_added", s, PER_SEQ["x_added"] - 16 + 2 * (t + 1)))
                        stats(s, 2 * TT + t + 1, t)
                    for t in range(4 * rnd, 4 * rnd + 4):
                        act.wait_ge(fin_ready, due("fin_ready", s, t + 1))
                        act.dma_start(out_t[s, t], X[:, t, :]).then_inc(out_stored, 16)
            act.wait_ge(out_stored, due("out_stored", SEQS, 0))

        @block.vector
        def _(dve):
            dve.sem_inc(y_sum, CREDIT["y_sum"])
            dve.sem_inc(y_ready, CREDIT["y_ready"])
            dve.sem_inc(x_added, CREDIT["x_added"])
            nc.vector.memset(eps[:, :], EPS).then_inc(eps_set, 1)
            chain = Chain(dve, dve_chain)
            V_ = nc.vector

            def rsqrt(s, n, t):
                dve.wait_ge(std_ready, due("std_ready", s, n))
                chain.link(V_.reciprocal(rstd[:, t:t + 1], std[:, t:t + 1]))

            def norm(s, which):
                x_now = x_first if which == 1 else X
                for t in range(TT + 1):
                    if t < TT:
                        rsqrt(s, 8 * (which - 1) + t + 1, t)
                        V_.scalar_tensor_tensor(out=xn[:, t % 2, :], in0=x_now[:, t, :], scalar=rstd[:, t:t + 1],
                                                in1=gain[:, :], op0=ALU.mult, op1=ALU.mult).then_inc(xn_ready, 1)
                    if t:
                        v = t - 1
                        for half in range(2):
                            b = PLAN.job[f"n{which}", v, half][0]
                            dve.wait_ge(hhi_ready, due("hhi_ready", s, 16 * (which - 1) + 2 * v + half + 1))
                            at_h = (slice(None), slice(4 * half, 4 * half + 4), slice(v * P, (v + 1) * P))
                            V_.tensor_tensor(h_lo[at_h], ps[:, b, :].rearrange("p (k q) -> p k q", q=P),
                                             h_hi[at_h].bitcast(F32), ALU.subtract).then_inc(h_ready, 1)

            partner = [i + 8 if i < 8 else i - 8 if i < 16 else i for i in range(32)]

            def rope_job(s, g, j):
                tile, half = order(g, j)
                if j:
                    dve.wait_ge(qk_ready, due("qk_ready", s, 8 * g + j))
                b, n = PLAN.job["proj", g, j]
                dve.wait_ge(bank_full[b], filled(s, b, n))
                tok = slice(half * H2, (half + 1) * H2)
                V_.tensor_tensor(r_c[:, :], ps[:, b, :], rope_sb[:, 0, tok], ALU.mult)
                chain.link(V_.stream_shuffle(r_sh[:, :], ps[:, b, :], partner))
                V_.tensor_tensor(r_s[:, :], r_sh[:, :], rope_sb[:, 1, tok], ALU.mult).then_inc(rope_read, 1)
                dve.wait_ge(rope_read, due("rope_read", s, 8 * g + j + 1))
                d = DIL[g]
                n = H2 // d
                V_.tensor_tensor(qk[g % 2][:, tile, :].rearrange("p (r i) -> p r i", r=d)[:, :, half * n:(half + 1) * n],
                                 r_c[:, :].rearrange("p (i r) -> p r i", r=d),
                                 r_s[:, :].rearrange("p (i r) -> p r i", r=d), ALU.add
                                 ).then_inc(qk_ready, 1)

            def softmax_unit(s, unit):
                _, wid, _, m = window(unit // UNITS, unit % TT)
                for h in range(2):
                    b, n = PLAN.job["s", unit, h]
                    dve.wait_ge(bank_full[b], filled(s, b, n))
                n = unit
                dve.wait_ge(p_ready, due("p_ready", s, n))
                mask = diag_sb[:, 0:wid] if m == 3 else masks_sb[:, m, 0:wid]
                V_.tensor_tensor(masked[:, :, 0:wid], ps[:, 4:6, 0:wid],
                                 mask.unsqueeze(1).broadcast_to([P, 2, wid]), ALU.add
                                 ).then_inc(s_read, 1)
                dve.wait_ge(s_read, due("s_read", s, n + 1))
                chain.link(V_.reduce_max(mx[:, :], masked[:, :, 0:wid], AX_X))
                if n >= 4:
                    dve.wait_ge(o_stored[n % 4], due(f"o_stored{n % 4}", s, n // 4))
                V_.tensor_scalar(o_st[:, n % 4, 2 * HEAD:2 * HEAD + 2], mx[:, :], -HEAD ** -0.5, None, ALU.mult
                                 ).then_inc(negmax_ready, 1)

            def pool_stage(s, what, g, first=0, last=0):
                n_before = POOL_GROUPS - g
                w, a = 2 << g, 8 - (1 << g)
                sums = [U[:, g, :], pw1, pw0, pw1, pw0]
                if what == "add":
                    if first == 0:
                        dve.wait_ge(u_ready, due("u_ready", s, 2 * n_before))
                    for k in range(first, last + 1):
                        n = T + 16 - (2 << k) + 1
                        chain.link(V_.tensor_tensor(sums[k + 1][:, 0:n], sums[k][:, 0:n],
                                                    sums[k][:, (1 << k):n + (1 << k)], ALU.add))
                elif what == "mean":
                    cur = sums[g + 1]
                    V_.tensor_tensor(cur[:, a:a + 8], cur[:, a:a + 8], edge_sb[:, g, 0:8], ALU.mult)
                    chain.link(V_.tensor_tensor(cur[:, a + 1016:a + 1024], cur[:, a + 1016:a + 1024],
                                                edge_sb[:, g, 8:16], ALU.mult))
                    V_.scalar_tensor_tensor(out=pooled[:, :], in0=cur[:, a:a + T], scalar=1.0 / w,
                                            in1=U[:, g, 8:8 + T], op0=ALU.mult, op1=ALU.subtract
                                            ).then_inc(pooled_ready, 1)
                else:
                    dve.wait_ge(pool_hi_ready, due("pool_hi_ready", s, n_before))
                    V_.tensor_tensor(pool_lo[:, :], pooled[:, :], pool_hi[:, :].bitcast(F32), ALU.subtract
                                     ).then_inc(pool_ready, 1)

            def merge(s, batch):
                dve.wait_ge(rec_in[batch], due(f"rec_in{batch}", s, 8))
                r = rec[batch]

                def heads(a):
                    return a.rearrange("p (t q h) -> p t q h", q=2, h=2)

                neg = [r[:, :, 2 * g:2 * g + 2, 2 * HEAD:2 * HEAD + 2] for g in range(GROUPS)]
                dens = [r[:, :, 2 * g:2 * g + 2, 2 * HEAD + 2:2 * HEAD + 4] for g in range(GROUPS)]
                chain.link(V_.tensor_tensor(heads(mn[:, :]), neg[0], neg[1], ALU.min))
                chain.link(V_.tensor_tensor(heads(mn[:, :]), heads(mn[:, :]), neg[2], ALU.min))
                for g in range(GROUPS):
                    ins = V_.tensor_tensor(heads(d3[:, g, :]), heads(mn[:, :]), neg[g], ALU.subtract)
                ins.then_inc(diff_ready, 1)
                dve.wait_ge(weight_ready, due("weight_ready", s, batch + 1))
                for g in range(GROUPS):
                    ins = V_.tensor_tensor(heads(wd[:, g, :]), heads(e3[:, g, :]), dens[g], ALU.mult)
                chain.link(ins)
                chain.link(V_.tensor_tensor(den[:, :], wd[:, 0, :], wd[:, 1, :], ALU.add))
                chain.link(V_.tensor_tensor(den[:, :], den[:, :], wd[:, 2, :], ALU.add))
                chain.link(V_.reciprocal(rden[:, :], den[:, :]))
                chain.link(V_.tensor_tensor(coef[:, :, :], e3[:, :, :],
                                            rden[:, :].unsqueeze(1).broadcast_to([P, 3, 16]), ALU.mult))
                for g in range(GROUPS):
                    for q in range(2):
                        o = r[:, :, 2 * g + q, 0:2 * HEAD].rearrange("p t (h e) -> p t h e", h=2)
                        c = heads(coef[:, g, :])[:, :, q, :].unsqueeze(3).broadcast_to([P, 4, 2, HEAD])
                        ins = V_.tensor_tensor(o, o, c, ALU.mult)
                chain.link(ins)
                total = r[:, :, 0:2, 0:2 * HEAD]
                chain.link(V_.tensor_tensor(total, total, r[:, :, 2:4, 0:2 * HEAD], ALU.add))
                V_.tensor_tensor(total, total, r[:, :, 4:6, 0:2 * HEAD], ALU.add).then_inc(merged, 1)

            def add_rows(s, i, fills0, fills_step, first, rnd):
                for idx in range(8 * rnd, 8 * rnd + 8):
                    b, t, n = idx % 8, idx // 2, idx % 2
                    dve.wait_ge(bank_full[b], filled(s, b, i * fills_step + (fills0[b] + first + idx // 8 + 1)))
                    xs = X[:, t, n * H2:(n + 1) * H2]
                    V_.tensor_tensor(xs, xs, ps[:, b, :], ALU.add).then_inc(x_added, 1)

            def y_low(s, j, half, n):
                dve.wait_ge(yhi_ready, due("yhi_ready", s, n))
                tok = slice(half * H2, (half + 1) * H2)
                V_.tensor_tensor(y_lo[j][:, tok], act_t[:, half, :], y_hi[j][:, tok].bitcast(F32), ALU.subtract
                                 ).then_inc(y_ready, 1)

            with dve.Fori(0, SEQS) as s:
                saved = chain.enter(s, DVE_STEPS)
                dve.wait_ge(gmix_in, due("gmix_in", s, 1))
                norm(s, 1)
                dve.wait_ge(const_in, 16 * 4)
                dve.wait_ge(tab_in, due("tab_in", s, 3))
                dve.wait_ge(out_stored, due("out_stored", s, 0))
                for j in range(8):
                    rope_job(s, 0, j)
                for unit in range(GROUPS * UNITS):
                    softmax_unit(s, unit)
                    for job in done(3 * unit - 3, 3 * unit - 1):
                        if job[0] == "proj" and job[2] < 8:
                            rope_job(s, job[1], job[2])
                    if unit == LAST:
                        V_.memset(U[:, :, 0:8], 0.0)
                        chain.link(V_.memset(U[:, :, 8 + T:16 + T], 0.0))
                    for stage in POOL_DVE.get(unit, ()):
                        pool_stage(s, *stage)
                pool_stage(s, "mean", 0)
                pool_stage(s, "lo", 0)

                def merged_low(j):
                    dve.wait_ge(mhi_ready, due("mhi_ready", s, j + 1))
                    tok = slice((j // 2) * H2, (j // 2 + 1) * H2)
                    V_.tensor_tensor(m_lo[:, j % 2, tok], ps[:, j, :], m_hi[:, j % 2, tok].bitcast(F32),
                                     ALU.subtract).then_inc(mT_ready, 1)

                merge(s, 0)
                merge(s, 1)
                for j in range(4):
                    merged_low(j)
                with dve.Fori(0, GATE_STEPS) as i:
                    for j in range(2):
                        f = i * 2 + j
                        for half in range(2):
                            dve.wait_ge(sig_ready, due("sig_ready", s, f * 4 + (half + 1)))
                            dve.wait_ge(bank_full[half], filled(s, half, i * GATE_FILLS + (PLAN.gate0[half] + j + 1)))
                            a = act_t[:, half, :]
                            V_.tensor_tensor(a, a, ps[:, half, :], ALU.mult).then_inc(a_read, 1)
                        for half in range(2):
                            dve.wait_ge(sig_ready, due("sig_ready", s, f * 4 + (half + 3)))
                            b = 2 + half
                            dve.wait_ge(bank_full[b], filled(s, b, i * GATE_FILLS + (PLAN.gate0[b] + j + 1)))
                            c = act_t[:, 2, :]
                            V_.tensor_tensor(c, c, ps[:, 2 + half, :], ALU.mult).then_inc(b_read, 1)
                            dve.wait_ge(b_read, due("b_read", s, f * 2 + (half + 1)))
                            a = act_t[:, half, :]
                            V_.tensor_tensor(a, a, c, ALU.add).then_inc(y_sum, 1)
                            y_low(s, j, half, f * 2 + (half + 1))
                    for t in range(TT):
                        dve.wait_ge(x_in[t], due(f"x_in{t}", s, 2))
                    for rnd in range(2):
                        add_rows(s, i, PLAN.gate0, GATE_FILLS, 2, rnd)
                dve.wait_ge(gffn_in, due("gffn_in", s, 1))
                norm(s, 2)

                def ffn_y(i):
                    for j in range(2):
                        for half in range(2):
                            b = 4 * j + 2 + half
                            dve.wait_ge(sig_ready, due("sig_ready", s, i * 4 + (32 + 2 * j + half + 1)))
                            dve.wait_ge(bank_full[b], filled(s, b, i * FFN_FILLS + (PLAN.ffn0[b] + 1)))
                            a = act_t[:, half, :]
                            V_.tensor_tensor(a, a, ps[:, b, :], ALU.mult).then_inc(y_sum, 1)
                        for half in range(2):
                            y_low(s, j, half, i * 4 + (16 + 2 * j + half + 1))

                with dve.Fori(0, FFN_STEPS - 1) as i:
                    ffn_y(i)
                    for rnd in range(2):
                        add_rows(s, i, PLAN.ffn0, FFN_FILLS, 1, rnd)
                ffn_y(FFN_STEPS - 1)
                dve.wait_ge(gfin_in, due("gfin_in", s, 1))
                for rnd in range(2):
                    add_rows(s, FFN_STEPS - 1, PLAN.ffn0, FFN_FILLS, 1, rnd)
                    for t in range(4 * rnd, 4 * rnd + 4):
                        rsqrt(s, 16 + t + 1, t)
                        V_.scalar_tensor_tensor(out=X[:, t, :], in0=X[:, t, :], scalar=rstd[:, t:t + 1],
                                                in1=g_fin[:, :], op0=ALU.mult, op1=ALU.mult
                                                ).then_inc(fin_ready, 1)
                chain.leave(saved, SEQS, DVE_STEPS)


def constants():
    inv = (THETA ** (-np.arange(ROPE_HALF, dtype=np.float32) / ROPE_HALF)).astype(np.float32)
    ang = np.arange(T, dtype=np.float32)[:, None] * inv[None, :]
    cos, sin = np.cos(ang.astype(np.float64)).T, np.sin(ang.astype(np.float64)).T
    rope = np.zeros((P, 2, T), np.float32)
    rope[:, 0] = 1.0
    for h in range(2):
        a, b = HEAD * h, HEAD * h + ROPE_HALF
        rope[a:b, 0], rope[b:b + ROPE_HALF, 0] = cos, cos
        rope[a:b, 1], rope[b:b + ROPE_HALF, 1] = -sin, sin
    q, k = np.arange(P)[:, None], np.arange(256)[None, :]
    masks = np.stack([np.where(np.abs(k - o - q) <= RADIUS, 0.0, -BIG) for o in (64, 0, 128)], 1)
    kk = np.arange(P)[None, :]
    diag = np.where(q % 2 == kk % 2, 0.0, -BIG)
    edge = np.ones((P, POOL_GROUPS, 16), np.float32)
    for g in range(POOL_GROUPS):
        w = 2 << g
        for c in range(16):
            i = c if c < 8 else T - 16 + c
            edge[:, g, c] = w / (min(i + w // 2, T) - max(i - w // 2, 0))
    return rope, masks.astype(np.float32), diag.astype(np.float32), np.eye(P, dtype=np.float32), edge


WEIGHTS = ("w_in", "pool_maps", "w_up_pool", "w_up_attn", "w_gate", "w_out", "w_ffn_gate", "w_ffn_up",
           "w_ffn_down", "norm_mix", "norm_ffn", "norm_final", "pool_scale", "b_gate")
COLUMNS = ("pool_scale", "b_gate")


def kernel(**inputs):
    import concourse.bacc as bacc
    from concourse.bass_utils import run_bass_kernel_spmd as run

    nc = bacc.Bacc("TRN2", target_bir_lowering=False, num_devices=1)
    arrays = {"x": np.concatenate([np.asarray(inputs["x_prompt"]), np.asarray(inputs["x_sample"])])}
    for name in WEIGHTS:
        a = np.asarray(inputs[name])
        a = a if name == "norm_final" else a[0]
        if name in COLUMNS:
            a = a.reshape(-1, P).T
        arrays[name] = np.ascontiguousarray(a)
    args = [nc.dram_tensor(n, a.shape, F32, kind="ExternalInput").ap() for n, a in arrays.items()]
    consts = [nc.inline_tensor(c, n).ap() for c, n in zip(constants(), ("rope", "masks", "diag", "ident", "edge"))]
    scratch = nc.dram_tensor("records", (2 * GROUPS, T, REC), F32, kind="Internal").ap()
    out = nc.dram_tensor("out", (SEQS, T, D), F32, kind="ExternalOutput").ap()
    encoder(nc, *args, *consts, scratch, out)
    r = run(nc, [arrays], core_ids=[0])
    y = r.results[0]["out"]
    return y[0:1], y[1:2]
```
